# Optimizing a Trainium2 kernel written in Bass

```python
import math
import jax, jax.numpy as jnp
from jax import lax
import numpy as np

D_MODEL = 1024
BATCH = 1
SEQ = 512
DEPTH = 1
DEC_BATCH = 8
DEC_SEQ = 8
PAST_LEN = 4096
PAGE_SIZE = 128

MIX_WIDTH = D_MODEL
ML_WIDTH = MIX_WIDTH // 2
ML_HEADS = 4
ML_HD = ML_WIDTH // ML_HEADS
ML_CHUNK = 64
CONV_W = 4
RW_WIDTH = MIX_WIDTH - ML_WIDTH
RW_HD = 64
RW_HEADS = RW_WIDTH // RW_HD
DECAY_LORA = 64
AAA_LORA = 64
GATE_LORA = 128
PEER_HEADS = 8
N_KEYS = 128
N_EXPERTS = N_KEYS * N_KEYS
PEER_QDIM = 256
PEER_TOPK = 16
PEER_BLOCK = 128
NORM_EPS = 1e-6
ML_NORM_EPS = 1e-6
GN_EPS = RW_HD * 1e-5
M_INIT = -1e30
ML_COLS = 4 * ML_WIDTH + 2 * ML_HEADS
RW_COLS = 3 * RW_WIDTH + DECAY_LORA + AAA_LORA + GATE_LORA
IN_COLS = ML_COLS + RW_COLS

kernel_name = 'hymba_mlstm_rwkv7_peer_step'

def rmsnorm(x, g):
    xf = x.astype(jnp.float32)
    y = xf * lax.rsqrt(jnp.mean(xf * xf, axis=-1, keepdims=True) + NORM_EPS)
    return (y * g.astype(jnp.float32)).astype(x.dtype)

def head_norm(y, g, eps):
    mu = jnp.mean(y, axis=-1, keepdims=True)
    var = jnp.mean(jnp.square(y - mu), axis=-1, keepdims=True)
    y = (y - mu) * lax.rsqrt(var + eps)
    return y.reshape(y.shape[:2] + (-1,)) * g

def mlstm_chunkwise(q, k, v, ig, lf, C0, n0, m0):
    B, H, T, DH = q.shape
    L = math.gcd(T, ML_CHUNK)
    nc = T // L
    to_chunks = lambda a: jnp.moveaxis(a.reshape((B, H, nc, L) + a.shape[3:]), 2, 0)
    causal = jnp.tril(jnp.ones((L, L), dtype=bool))

    def chunk_step(carry, inp):
        C, n, m = carry
        qc, kc, vc, ic, fc = inp
        b = jnp.cumsum(fc, axis=-1)
        log_d = jnp.where(causal, b[..., :, None] - b[..., None, :] + ic[..., None, :], -jnp.inf)
        log_inter = b + m[..., None]
        m_t = jnp.maximum(log_inter, jnp.max(log_d, axis=-1))
        d = jnp.exp(log_d - m_t[..., None])
        s_inter = jnp.exp(log_inter - m_t)
        qk = jnp.einsum('bhtd,bhsd->bhts', qc, kc) * d
        num = s_inter[..., None] * jnp.einsum('bhtd,bhde->bhte', qc, C) + jnp.einsum('bhts,bhse->bhte', qk, vc)
        den = s_inter * jnp.einsum('bhtd,bhd->bht', qc, n) + jnp.sum(qk, axis=-1)
        h = num / jnp.maximum(jnp.abs(den), jnp.exp(-m_t))[..., None]
        m_new = m_t[..., -1]
        s_state = jnp.exp(b[..., -1] + m - m_new)
        w_chunk = jnp.exp(b[..., -1:] - b + ic - m_new[..., None])
        C_new = s_state[..., None, None] * C + jnp.einsum('bhs,bhsd,bhse->bhde', w_chunk, kc, vc)
        n_new = s_state[..., None] * n + jnp.einsum('bhs,bhsd->bhd', w_chunk, kc)
        return (C_new, n_new, m_new), h

    (C1, n1, m1), hs = lax.scan(chunk_step, (C0, n0, m0), tuple(to_chunks(a) for a in (q, k, v, ig, lf)))
    h = jnp.moveaxis(hs, 0, 2).reshape(B, H, T, DH)
    return h, C1, n1, m1

def mlstm_mixer(cols, conv0, C0, n0, m0, conv_w, conv_b, b_i, b_f, norm_g):
    B, T, _ = cols.shape
    qk_raw = cols[..., :2 * ML_WIDTH]
    v = cols[..., 2 * ML_WIDTH:3 * ML_WIDTH]
    o = cols[..., 3 * ML_WIDTH:4 * ML_WIDTH]
    ig = cols[..., 4 * ML_WIDTH:4 * ML_WIDTH + ML_HEADS] + b_i
    fg = cols[..., 4 * ML_WIDTH + ML_HEADS:] + b_f
    ext = jnp.concatenate([conv0, qk_raw], axis=1)
    qk = conv_b + sum(ext[:, j:j + T] * conv_w[j] for j in range(CONV_W))
    qk = jax.nn.silu(qk)
    heads = lambda a: a.reshape(B, T, ML_HEADS, ML_HD).transpose(0, 2, 1, 3)
    q = heads(qk[..., :ML_WIDTH])
    k = heads(qk[..., ML_WIDTH:]) * (ML_HD ** -0.5)
    h, C1, n1, m1 = mlstm_chunkwise(q, k, heads(v), ig.transpose(0, 2, 1),
                                    jax.nn.log_sigmoid(fg).transpose(0, 2, 1), C0, n0, m0)
    h = head_norm(h.transpose(0, 2, 1, 3), norm_g, ML_NORM_EPS) * jax.nn.sigmoid(o)
    return h, C1, n1, m1, ext[:, T:]

def rwkv7_mixer(cols, shift0, S0, mu, w0, w2, a0, a2, g2, k_k, k_a, r_k, gn_g, gn_b):
    B, T, _ = cols.shape
    W = RW_WIDTH
    prev = jnp.concatenate([shift0[:, None, :], cols[:, :-1]], axis=1)
    xs = cols + (prev - cols) * mu
    r, k, v = xs[..., :W], xs[..., W:2 * W], xs[..., 2 * W:3 * W]
    wd = xs[..., 3 * W:3 * W + DECAY_LORA]
    ad = xs[..., 3 * W + DECAY_LORA:3 * W + DECAY_LORA + AAA_LORA]
    gd = xs[..., 3 * W + DECAY_LORA + AAA_LORA:]
    w_log = -jax.nn.softplus(-(w0 + jnp.tanh(wd) @ w2)) - 0.5
    decay = jnp.exp(-jnp.exp(w_log))
    a = jax.nn.sigmoid(a0 + ad @ a2)
    g = jax.nn.sigmoid(gd) @ g2
    kk = k * k_k
    k = k * (1.0 + (a - 1.0) * k_a)
    heads = lambda t: t.reshape(B, T, RW_HEADS, RW_HD)
    r, k, v, kk, a, decay = map(heads, (r, k, v, kk, a, decay))
    kk = kk / jnp.maximum(jnp.linalg.norm(kk, axis=-1, keepdims=True), 1e-12)

    def step(S, inp):
        rt, wt, kt, vt, kkt, at = inp
        sa = jnp.einsum('bhvk,bhk->bhv', S, -kkt)
        S = S * wt[:, :, None, :] + sa[..., None] * (kkt * at)[:, :, None, :] + vt[..., None] * kt[:, :, None, :]
        return S, jnp.einsum('bhvk,bhk->bhv', S, rt)

    S1, ys = lax.scan(step, S0, tuple(jnp.swapaxes(t, 0, 1) for t in (r, decay, k, v, kk, a)))
    y = head_norm(jnp.swapaxes(ys, 0, 1), gn_g, GN_EPS) + gn_b
    y = y + (jnp.sum(r * k * r_k, axis=-1, keepdims=True) * v).reshape(B, T, W)
    return y * g, S1, cols[:, -1]

def peer(h, w_q, sub_keys, u_emb, v_emb):
    B, T, D = h.shape
    n = B * T
    n_blocks = -(-n // PEER_BLOCK)
    flat = jnp.pad(h.reshape(n, D), ((0, n_blocks * PEER_BLOCK - n), (0, 0))).reshape(n_blocks, PEER_BLOCK, D)

    def block(xb):
        q = (xb @ w_q).astype(jnp.float32).reshape(PEER_BLOCK, PEER_HEADS, 2, PEER_QDIM // 2)
        s = jnp.einsum('bhpd,hpkd->bhpk', q, sub_keys.astype(jnp.float32))
        sv, si = lax.top_k(s, PEER_TOPK)
        cand = (sv[:, :, 0, :, None] + sv[:, :, 1, None, :]).reshape(PEER_BLOCK, PEER_HEADS, PEER_TOPK * PEER_TOPK)
        cv, ci = lax.top_k(cand, PEER_TOPK)
        i1 = jnp.take_along_axis(si[:, :, 0], ci // PEER_TOPK, axis=-1)
        i2 = jnp.take_along_axis(si[:, :, 1], ci % PEER_TOPK, axis=-1)
        idx = i1 * N_KEYS + i2
        gate = jax.nn.softmax(cv, axis=-1)
        act = jax.nn.gelu(jnp.einsum('bhkd,bd->bhk', u_emb[idx], xb).astype(jnp.float32), approximate=False)
        return jnp.einsum('bhk,bhkd->bd', (gate * act).astype(v_emb.dtype), v_emb[idx])

    out = lax.map(block, flat)
    return out.reshape(-1, D)[:n].reshape(B, T, D).astype(h.dtype)

def hybrid_layer(x, C0, n0, m0, conv0, S0, shift0,
                 norm_mix_g, w_in, ml_conv_w, ml_conv_b, ml_b_i, ml_b_f, ml_norm_g,
                 rw_mu, rw_w0, rw_w2, rw_a0, rw_a2, rw_g2, rw_k_k, rw_k_a, rw_r_k, rw_gn_g, rw_gn_b,
                 w_out, norm_ffn_g, peer_w_q, peer_sub_keys, peer_u, peer_v):
    f32 = jnp.float32
    cols = (rmsnorm(x, norm_mix_g) @ w_in).astype(f32)
    ml_out, C1, n1, m1, conv1 = mlstm_mixer(cols[..., :ML_COLS], conv0.astype(f32), C0.astype(f32),
                                            n0.astype(f32), m0.astype(f32), ml_conv_w, ml_conv_b,
                                            ml_b_i, ml_b_f, ml_norm_g)
    rw_out, S1, shift1 = rwkv7_mixer(cols[..., ML_COLS:], shift0.astype(f32), S0.astype(f32), rw_mu,
                                     rw_w0, rw_w2, rw_a0, rw_a2, rw_g2, rw_k_k, rw_k_a, rw_r_k,
                                     rw_gn_g, rw_gn_b)
    mix = jnp.concatenate([ml_out, rw_out], axis=-1).astype(x.dtype)
    x = x + mix @ w_out
    x = x + peer(rmsnorm(x, norm_ffn_g), peer_w_q, peer_sub_keys, peer_u, peer_v)
    return x, (C1, n1, m1, conv1, S1, shift1)

def trunk(x, states, layer_weights, norm_final_g):
    new = [[] for _ in states]
    for l in range(DEPTH):
        lw = [w[l] for w in layer_weights]
        x, st = hybrid_layer(x, *[s[l] for s in states], *lw)
        for lst, s_new, s_old in zip(new, st, states):
            lst.append(s_new.astype(s_old.dtype))
    return rmsnorm(x, norm_final_g), [jnp.stack(lst) for lst in new]

def setup_inputs(seed: int = 0) -> dict:
    key = jax.random.key(seed)
    ks = iter(jax.random.split(key, 40))
    nrm = lambda shape, scale: scale * jax.random.normal(next(ks), shape, jnp.float32)
    unif = lambda shape, lo, hi: jax.random.uniform(next(ks), shape, jnp.float32, lo, hi)
    L = DEPTH
    return {
        'x_prompt': nrm((BATCH, SEQ, D_MODEL), 1.0),
        'x_sample': nrm((DEC_BATCH, DEC_SEQ, D_MODEL), 1.0),
        'state_mlstm_C': nrm((L, DEC_BATCH, ML_HEADS, ML_HD, ML_HD), 0.05),
        'state_mlstm_n': nrm((L, DEC_BATCH, ML_HEADS, ML_HD), 0.5),
        'state_mlstm_m': nrm((L, DEC_BATCH, ML_HEADS), 1.0),
        'state_mlstm_conv': nrm((L, DEC_BATCH, CONV_W - 1, 2 * ML_WIDTH), 1.0),
        'state_rwkv_S': nrm((L, DEC_BATCH, RW_HEADS, RW_HD, RW_HD), 0.3),
        'state_rwkv_shift': nrm((L, DEC_BATCH, RW_COLS), 1.0),
        'norm_mix_g': 1.0 + nrm((L, D_MODEL), 0.02),
        'w_in': nrm((L, D_MODEL, IN_COLS), D_MODEL ** -0.5),
        'ml_conv_w': nrm((L, CONV_W, 2 * ML_WIDTH), 0.5),
        'ml_conv_b': nrm((L, 2 * ML_WIDTH), 0.02),
        'ml_b_i': nrm((L, ML_HEADS), 0.1),
        'ml_b_f': unif((L, ML_HEADS), 3.0, 6.0),
        'ml_norm_g': 1.0 + nrm((L, ML_WIDTH), 0.02),
        'rw_mu': unif((L, RW_COLS), 0.0, 1.0),
        'rw_w0': unif((L, RW_WIDTH), -6.0, 1.0),
        'rw_w2': nrm((L, DECAY_LORA, RW_WIDTH), 0.1),
        'rw_a0': nrm((L, RW_WIDTH), 0.1),
        'rw_a2': nrm((L, AAA_LORA, RW_WIDTH), 0.1),
        'rw_g2': nrm((L, GATE_LORA, RW_WIDTH), GATE_LORA ** -0.5),
        'rw_k_k': 0.85 + nrm((L, RW_WIDTH), 0.02),
        'rw_k_a': 1.0 + nrm((L, RW_WIDTH), 0.02),
        'rw_r_k': nrm((L, RW_HEADS, RW_HD), 0.1),
        'rw_gn_g': 1.0 + nrm((L, RW_WIDTH), 0.02),
        'rw_gn_b': nrm((L, RW_WIDTH), 0.02),
        'w_out': nrm((L, MIX_WIDTH, D_MODEL), MIX_WIDTH ** -0.5),
        'norm_ffn_g': 1.0 + nrm((L, D_MODEL), 0.02),
        'peer_w_q': nrm((L, D_MODEL, PEER_HEADS * PEER_QDIM), D_MODEL ** -0.5),
        'peer_sub_keys': nrm((L, PEER_HEADS, 2, N_KEYS, PEER_QDIM // 2), (PEER_QDIM // 2) ** -0.5),
        'peer_u': nrm((L, N_EXPERTS, D_MODEL), D_MODEL ** -0.5),
        'peer_v': nrm((L, N_EXPERTS, D_MODEL), PEER_HEADS ** -0.5),
        'norm_final_g': 1.0 + nrm((D_MODEL,), 0.02),
    }

def reference(x_prompt, x_sample, state_mlstm_C, state_mlstm_n, state_mlstm_m, state_mlstm_conv,
              state_rwkv_S, state_rwkv_shift,
              norm_mix_g, w_in, ml_conv_w, ml_conv_b, ml_b_i, ml_b_f, ml_norm_g,
              rw_mu, rw_w0, rw_w2, rw_a0, rw_a2, rw_g2, rw_k_k, rw_k_a, rw_r_k, rw_gn_g, rw_gn_b,
              w_out, norm_ffn_g, peer_w_q, peer_sub_keys, peer_u, peer_v, norm_final_g):
    layer_weights = (norm_mix_g, w_in, ml_conv_w, ml_conv_b, ml_b_i, ml_b_f, ml_norm_g,
                     rw_mu, rw_w0, rw_w2, rw_a0, rw_a2, rw_g2, rw_k_k, rw_k_a, rw_r_k, rw_gn_g, rw_gn_b,
                     w_out, norm_ffn_g, peer_w_q, peer_sub_keys, peer_u, peer_v)
    f32 = jnp.float32
    z = lambda *s: jnp.zeros((DEPTH, BATCH) + s, f32)
    prompt_states = (z(ML_HEADS, ML_HD, ML_HD), z(ML_HEADS, ML_HD),
                     jnp.full((DEPTH, BATCH, ML_HEADS), M_INIT, f32), z(CONV_W - 1, 2 * ML_WIDTH),
                     z(RW_HEADS, RW_HD, RW_HD), z(RW_COLS))
    sample_states = (state_mlstm_C, state_mlstm_n, state_mlstm_m, state_mlstm_conv,
                     state_rwkv_S, state_rwkv_shift)
    y_prompt, (p_C, p_n, p_m, p_conv, p_S, p_shift) = trunk(x_prompt, prompt_states, layer_weights, norm_final_g)
    y_sample, (s_C, s_n, s_m, s_conv, s_S, s_shift) = trunk(x_sample, sample_states, layer_weights, norm_final_g)
    return (y_prompt, y_sample, p_C, p_n, p_m, p_conv, p_S, p_shift, s_C, s_n, s_m, s_conv, s_S, s_shift)


_drawn_inputs = setup_inputs


def setup_inputs(seed=0):
    import zlib

    import numpy as np

    out = dict(_drawn_inputs(seed))
    spreads = {}
    factors = {'ml_norm_g': 46.742,
     'rw_k_a': 2.697,
     'rw_gn_g': 44.13,
     'rw_gn_b': 42.78,
     'norm_final_g': 20.362,
     'rw_k_k': 8.036,
     'norm_ffn_g': 19.259,
     'rw_r_k': 3.825}
    for name, (base, spread) in spreads.items():
        noise = np.random.default_rng([zlib.crc32(name.encode()), seed]).standard_normal(out[name].shape)
        drawn = base * np.exp(spread * noise) if base else spread * noise
        out[name] = __import__('jax').numpy.asarray(drawn.astype(out[name].dtype))
    for name, factor in factors.items():
        out[name] = (out[name] * factor).astype(out[name].dtype)
    return out
```

```python
import concourse.bass as bass
from concourse import mybir
from contextlib import ExitStack
import math

D = 1024
SEQ = 512
NB, NS = 8, 8
SAMP = NB * NS
NT = SEQ + SAMP
KD = D // 128
MLH = 4
NE = 128 * 128
PT = SEQ // 128
TILES = [(t * 128, 128) for t in range(PT)] + [(SEQ, SAMP)]
MCH = 128
RCH = 64
CW = 4
RT_TILES = 14
EXQ = 3 + SEQ + NB * (NS + 3)
EXR = 1 + SEQ + NB * (NS + 1)
HEADS, TOPK = 8, 16
RING = 8
LEAD = 32
NEG = -1.0e30
ML_END = 2056
PCOL = {}
_at = 0
for _n, _w in [("g_mix", 8), ("conv_w", 32), ("conv_b", 8), ("ml_g", 4), ("mu", 14), ("w0", 4), ("a0", 4),
               ("k_k", 4), ("k_a", 4), ("r_k", 4), ("gn_g", 4), ("gn_b", 4)]:
    PCOL[_n] = _at
    _at += _w
NPAR = _at


def hybrid_step(nc, xT_d, x_d, par_d, small_d, conv0_d, shift0_d, cn0_d, s0_d, w_in, w2_d, a2_d, g2_d,
                w_out, gffn_d, gfin_d, w_q, sub_d, pu, pv,
                y_o, cn_p_o, m_o, conv_o, s_p_o, shift_o, cn_s_o, s_s_o):
    f32 = mybir.dt.float32
    u32 = mybir.dt.uint32
    ALU = mybir.AluOpType
    ACT = mybir.ActivationFunctionType
    AX = mybir.AxisListType

    ctx = ExitStack()
    with ctx:
        def sb(name, shape, dt=f32, scope=ctx):
            return scope.enter_context(nc.sbuf_tensor(name, shape, dt))

        def sem(name):
            return ctx.enter_context(nc.semaphore(name))

        bank = [ctx.enter_context(nc.psum_tensor(f"bank{i}", [128, 512], f32)) for i in range(8)]

        ident = sb("ident", [128, 128])
        ones = sb("ones", [128, 128])
        mixT = sb("mixT", [128, KD, NT])
        eps_t = sb("eps_t", [128, 4])
        mixers = ExitStack()
        blk = sb("blk", [128, 128], scope=mixers)
        id64 = sb("id64", [128, 64], scope=mixers)
        negm = sb("negm", [128, 128], scope=mixers)
        negs = sb("negs", [64, 64], scope=mixers)
        seqm = sb("seqm", [64, NB], scope=mixers)
        mask4 = sb("mask4", [128, 4, 128], scope=mixers)
        mask4s = sb("mask4s", [64, 4, 64], scope=mixers)
        mask3 = sb("mask3", [128, 3, 128], scope=mixers)
        masks = sb("masks", [64, 64], scope=mixers)
        mtmp = sb("mtmp", [128, 3, 128], scope=mixers)
        selr = sb("selr", [4, MLH, 128], scope=mixers)
        rst_m = sb("rst_m", [4, NT], scope=mixers)
        rst_r = sb("rst_r", [128, NT], scope=mixers)
        par = sb("par", [128, NPAR], scope=mixers)
        small = sb("small", [4, 2 + NB], scope=mixers)
        cn0 = sb("cn0", [128, NB, MLH, 129], scope=mixers)
        s0 = sb("s0", [128, NB, 4, 64], scope=mixers)
        w2 = sb("w2", [64, 512], scope=mixers)
        a2 = sb("a2", [128, 512], scope=mixers)
        g2 = sb("g2", [128, 512], scope=mixers)
        ext_r = sb("ext_r", [128, RT_TILES, EXR], scope=mixers)
        shift_t = sb("shift_t", [128, RT_TILES, 1 + NB], scope=mixers)
        mlstm = ExitStack()
        ext_q = sb("ext_q", [128, 8, EXQ], scope=mlstm)
        vaug = sb("vaug", [128, 5, MLH, 129], scope=mlstm)
        osig = sb("osig", [128, MLH, NT], scope=mlstm)
        gi = sb("gi", [4, NT], scope=mlstm)
        gf = sb("gf", [4, NT], scope=mlstm)
        conv_t = sb("conv_t", [128, 8, 1 + NB, 3], scope=mlstm)
        proj = ExitStack()
        xnT = sb("xnT", [128, KD, NT], scope=proj)
        wbuf = [sb(f"wbuf{i}", [128, KD, 512], scope=proj) for i in range(2)]
        conv0 = sb("conv0", [128, 8, NB, 3], scope=proj)
        shift0 = sb("shift0", [128, RT_TILES, NB], scope=proj)
        rb = sb("rb", [128, NT], scope=proj)
        sq = sb("sq", [128, 2, NT], scope=proj)
        proj.close()
        mw = ExitStack()
        rows = {n: sb("row_" + n, [4, NT], scope=mw) for n in ["l", "b", "m", "E1", "E2", "Ks", "W", "flo"]}
        mo = sb("mo", [4, 1 + NB], scope=mw)
        mcol = sb("mcol", [128, 5, 2, 4], scope=mw)
        wcolX = sb("wcolX", [64, MLH, NB], scope=mw)
        pre = sb("pre", [128, 2, NT], scope=mw)
        sg = sb("sg", [128, 2, NT], scope=mw)
        qh = sb("qh", [128, NT], scope=mw)
        kh = sb("kh", [128, NT], scope=mw)
        qs = sb("qs", [128, NT], scope=mw)
        qn = sb("qn", [128, NT], scope=mw)
        bc = sb("bc", [128, 3, NT], scope=mw)
        ktok = sb("ktok", [128, 5, 128], scope=mw)
        dmat = sb("dmat", [128, 5, 128], scope=mw)
        pmat = sb("pmat", [128, 5, 128], scope=mw)
        wv = sb("wv", [128, PT, 129], scope=mw)
        wvX = sb("wvX", [64, NB, 129], scope=mw)
        cn = sb("cn", [128, PT, 129], scope=mw)
        cnS = sb("cnS", [128, NB, 129], scope=mw)
        hb, hq, hr = pre[:, 0, :], pre[:, 1, :], sg[:, 0, :]
        mw.close()
        mlstm.close()
        rwk = ExitStack()
        xwa = sb("xwa", [128, NT], scope=rwk)
        xg = sb("xg", [128, NT], scope=rwk)
        X = {n: sb("rw_" + n, [128, NT], scope=rwk) for n in
             ["d", "r", "k", "v", "sw", "av", "gv", "cum", "cm", "Ep", "En", "kk", "t", "kf",
              "be", "ka", "bv", "reff", "y"]}
        AR = sb("rw_AR", [128, 2, NT], scope=rwk)
        tok4 = sb("tok4", [128, 2, 4, 128], scope=rwk)
        G4 = [sb(f"G4_{u}", [128, 4, 128], scope=rwk) for u in range(4)]
        M3 = [sb(f"M3_{u}", [128, 3, 128], scope=rwk) for u in range(4)]
        XM = [[sb(f"XM{u}_{i}", [128, 3, 128], scope=rwk) for i in range(2)] for u in range(4)]
        TB = [sb(f"TB{u}", [128, 2, 128], scope=rwk) for u in range(4)]
        NV = [sb(f"NV{u}", [128, 64], scope=rwk) for u in range(4)]
        TS = [sb(f"TS{u}", [128, 128], scope=rwk) for u in range(4)]
        bX = sb("bX", [64, NB, 128], scope=rwk)
        kX = sb("kX", [64, NB, 128], scope=rwk)
        Gt = sb("Gt", [128, 8, 64], scope=rwk)
        PH = sb("PH", [128, 8, 64], scope=rwk)
        GtS = sb("GtS", [128, 8, 64], scope=rwk)
        PHS = sb("PHS", [128, 8, 64], scope=rwk)
        Sst = sb("Sst", [128, 8, 64], scope=rwk)
        SsS = sb("SsS", [128, 8, 64], scope=rwk)
        rwk.close()
        mixers.close()
        pe_sc = ExitStack()
        xf = sb("xf", [128, 5, D], scope=pe_sc)
        x1 = sb("x1", [128, 5, D], scope=pe_sc)
        gb = sb("gb", [128, 2, D], scope=pe_sc)
        idx = sb("idx", [128, 5, HEADS * TOPK], u32, scope=pe_sc)
        gate = sb("gate", [128, 5, HEADS * TOPK], scope=pe_sc)
        st = sb("st", [128, 5, 4], scope=pe_sc)
        route = ExitStack()
        wo = sb("wo", [128, KD, 512], scope=route)
        xfT = sb("xfT", [128, KD, NT], scope=route)
        wq = [sb("wqa", [128, KD, 512], scope=route), wo]
        qT = sb("qT", [128, 16, NT], scope=route)
        subT = sb("subT", [128, 16, 128], scope=route)
        sc = sb("sc", [128, 2048], scope=route)
        sc2 = sb("sc2", [128, 2048], scope=route)
        sv = sb("sv", [128, 16, 16], scope=route)
        si = sb("si", [128, 16, 16], u32, scope=route)
        sif = sb("sif", [128, 16, 16], scope=route)
        cv = sb("cv", [128, HEADS, 16], scope=route)
        ci = sb("ci", [128, HEADS, 16], u32, scope=route)
        cab = sb("cab", [128, 2, HEADS * 16], u32, scope=route)
        cabf = sb("cabf", [128, 2, HEADS * 16], scope=route)
        isel = sb("isel", [128, 2, HEADS * 16], scope=route)
        io16 = sb("io16", [128, 16], scope=route)
        mx8 = sb("mx8", [128, 2, HEADS], scope=route)
        route.close()
        gat = ExitStack()
        ub = sb("ub", [128, RING, D], scope=gat)
        vb = sb("vb", [128, RING, D], scope=gat)
        diag = sb("diag", [128, 16, 128], scope=gat)
        ucol = sb("ucol", [128, 2, 16], u32, scope=gat)
        dots = sb("dots", [128, 2, 16], scope=gat)
        gel = sb("gel", [128, 2, 16], scope=gat)
        wts = sb("wts", [128, 2, 16], scope=gat)
        junk = sb("junk", [128, D], scope=gat)
        zer = sb("zer", [128, 512], scope=gat)
        gat.close()
        pe_sc.close()

        def pcol(name, t):
            return par[:, PCOL[name] + t:PCOL[name] + t + 1]

        s_par, s_x, s_w, s_init = sem("par_loaded"), sem("xT_loaded"), [sem("w_loaded0"), sem("w_loaded1")], sem("state_loaded")
        s_out = sem("stores_done")
        s_wo = sem("wout_loaded")
        s_x1 = sem("x_loaded")
        s_wq = [sem("wq_loaded0"), sem("wq_loaded1")]
        s_sub = sem("subkeys_loaded")
        c_dve, c_act, c_pool = sem("vector_step"), sem("scalar_step"), sem("gpsimd_step")
        s_const = sem("constants_ready")
        s_sq, s_sqf, s_sd, s_xn = sem("squares_ready"), sem("squares_summed"), sem("rms_ready"), sem("xn_ready")
        s_pj, s_pe = sem("proj_done"), sem("proj_copied")
        held = {}

        def S(name):
            if name not in held:
                held[name] = sem(name)
            return held[name]

        block = ctx.enter_context(nc.Block())

        PANELS = [(0, 512), (512, 512), (1024, 512), (1536, 512), (2048, 8),
                  (ML_END, 512), (ML_END + 512, 512), (ML_END + 1024, 512), (ML_END + 1536, 256)]
        JOBS = []
        for p in (0, 1):
            JOBS += [("q", p, 128 * j, 128, 4 * p + j) for j in range(4)]
        JOBS += [("v", 2, 0, 512, t) for t in range(5)]
        JOBS += [("o", 3, 128 * j, 128, j) for j in range(4)]
        JOBS += [("i", 4, 0, 4, 0), ("f", 4, 4, 4, 0)]
        for p in range(5, 9):
            JOBS += [("r", p, 128 * j, 128, 4 * (p - 5) + j) for j in range(PANELS[p][1] // 128)]
        NJ = len(JOBS)

        def main_samp(ap):
            return [ap[:, 0:SEQ], ap[:, SEQ:NT]]

        GROUPS = [[0, 1], [2, 3], [4]]

        def units(g):
            return [(t, h) for t in GROUPS[g] for h in range(2)]

        ULIST = [(p, g, u) for p in range(4) for g in range(3) for u in range(len(units(g)))]

        @block.sync
        def _(sp):
            sp.dma_start(par[:, :], par_d).then_inc(s_par, 16)
            sp.dma_start(xnT[:, :, :], xT_d.rearrange("(k p) n -> p k n", p=128)).then_inc(s_x, 16)
            for p, (c0, w) in enumerate(PANELS):
                if p >= 2:
                    sp.wait_ge(s_pj, sum(j[1] <= p - 2 for j in JOBS))
                sp.dma_start(wbuf[p % 2][:, :, 0:w],
                             w_in.rearrange("(k p) n -> p k n", p=128)[:, :, c0:c0 + w]).then_inc(s_w[p % 2], 16)
                if p == 1:
                    for dst, src in [(small[:, :], small_d), (conv0[:, :, :, :], conv0_d), (shift0[:, :, :], shift0_d),
                                     (cn0[:, :, :, :], cn0_d), (s0[:, :, :, :], s0_d), (w2[:, :], w2_d),
                                     (a2[64:128, :], a2_d), (g2[:, :], g2_d)]:
                        sp.dma_start(dst, src).then_inc(s_init, 16)
            sp.wait_ge(S("m_ready"), 1)
            sp.dma_start(m_o, mo[:, :]).then_inc(s_out, 16)
            for h in range(MLH):
                sp.wait_ge(S("cn_ready"), h + 1)
                sp.dma_start(cn_p_o[:, h, :], cn[:, PT - 1, :]).then_inc(s_out, 16)
                sp.dma_start(cn_s_o[:, h, :, :], cnS[:, :, :]).then_inc(s_out, 16)
            sp.wait_ge(S("tails_ready"), 2)
            sp.dma_start(conv_o, conv_t[:, :, :, :]).then_inc(s_out, 16)
            sp.dma_start(shift_o, shift_t[:, :, :]).then_inc(s_out, 16)
            for p in range(4):
                sp.wait_ge(S("rstate_ready"), p + 1)
                sp.dma_start(s_p_o[:, p, :], Sst[:, 7, :]).then_inc(s_out, 16)
                sp.dma_start(s_s_o[:, p, :, :], SsS[:, :, :]).then_inc(s_out, 16)
            sp.wait_ge(S("mix_ready"), 8)
            sp.wait_ge(s_out, 16 * 19)
            for t, (t0, n) in enumerate(TILES):
                sp.dma_start(x1[0:n, t, :], x_d[t0:t0 + n, :]).then_inc(s_x1, 16)
            sp.dma_start(gb[:, 0, :], gffn_d.partition_broadcast(128)).then_inc(s_x1, 16)
            sp.dma_start(gb[:, 1, :], gfin_d.partition_broadcast(128)).then_inc(s_x1, 16)
            sp.dma_start(subT[:, :, :], sub_d).then_inc(s_sub, 16)
            for half in range(2):
                if half:
                    sp.wait_ge(S("outproj_done"), 5)
                sp.dma_start(wo[:, :, :], w_out.rearrange("(k p) n -> p k n", p=128)[:, :, 512 * half:512 * half + 512]
                             ).then_inc(s_wo, 16)
            for p in range(4):
                if p == 1:
                    sp.wait_ge(S("outproj_done"), 10)
                if p >= 2:
                    sp.wait_ge(S("qproj_done"), 4 * (p - 1))
                sp.dma_start(wq[p % 2][:, :, :], w_q.rearrange("(k p) n -> p k n", p=128)[:, :, 512 * p:512 * p + 512]
                             ).then_inc(s_wq[p % 2], 16)
            for t, (t0, n) in enumerate(TILES):
                sp.wait_ge(S("y_ready"), t + 1)
                sp.dma_start(y_o[t0:t0 + n, :], x1[0:n, t, :]).then_inc(s_out, 16)
            sp.wait_ge(s_out, 16 * (19 + 5))

        @block.gpsimd
        def _(pool):
            k = [0]

            def link(ins):
                k[0] += 1
                ins.then_inc(c_pool, 1)
                pool.wait_ge(c_pool, k[0])

            def select(out, pattern, base, mult, fill, op=ALU.is_ge):
                link(pool.affine_select(out=out, in_=out, compare_op=op, fill=fill, base=base,
                                        pattern=pattern, channel_multiplier=mult))

            link(pool.memset(ident[:, :], 0.0))
            select(ident[:, :], [[-1, 128]], 0, 1, 1.0, ALU.not_equal)
            link(pool.memset(ones[:, :], 1.0))
            link(pool.memset(eps_t[:, 0:1], 1e-6))
            link(pool.memset(eps_t[:, 1:2], 64 * 1e-5))
            link(pool.memset(eps_t[:, 2:3], 1.0))
            pool.memset(eps_t[:, 3:4], 0.0).then_inc(s_const, 1)
            link(pool.memset(ext_q[:, :, 0:3], 0.0))
            link(pool.memset(ext_r[:, :, 0:1], 0.0))
            link(pool.memset(vaug[:, :, :, 128:129], 1.0))
            def block_ones(out, p, n, w):
                link(pool.memset(out, 1.0))
                v = out.rearrange("p (c w) -> p c w", w=w)
                select(v, [[-w, n // w], [0, w]], 0, 1, 0.0)
                select(v, [[w, n // w], [0, w]], w - 1, -1, 0.0)
            block_ones(blk[:, :], 128, 128, 64)
            link(pool.memset(id64[:, :], 0.0))
            select(id64[:, :], [[-1, 64]], 0, 1, 1.0, ALU.not_equal)
            select(id64[:, :], [[-1, 64]], -64, 1, 1.0, ALU.not_equal)
            link(pool.memset(negm[:, :], 0.0))
            select(negm[:, :], [[1, 128]], 0, -1, NEG)
            link(pool.memset(negs[:, :], 0.0))
            select(negs[:, :], [[1, 64]], 0, -1, NEG)
            select(negs[:, :].rearrange("p (c w) -> p c w", w=8), [[-8, 8], [0, 8]], 0, 1, NEG)
            select(negs[:, :].rearrange("p (c w) -> p c w", w=8), [[8, 8], [0, 8]], 7, -1, NEG)
            link(pool.memset(seqm[:, :], 1.0))
            select(seqm[:, :], [[-8, 8]], 0, 1, 0.0)
            select(seqm[:, :], [[8, 8]], 7, -1, 0.0)
            for i, w in enumerate((16, 32, 64)):
                block_ones(mtmp[:, i, :], 128, 128, w)
            for i in range(3):
                link(pool.tensor_copy(mask3[:, i, :], mtmp[:, i, :]))
            for i in (1, 2):
                link(pool.tensor_tensor(mask3[:, i, :], mtmp[:, i, :], mtmp[:, i - 1, :], ALU.subtract))
            select(mask3[:, :, :], [[0, 3], [-1, 128]], -1, 1, 0.0)
            link(pool.tensor_copy(mask4[:, 0, :], mtmp[:, 0, :]))
            for i in (1, 2, 3):
                link(pool.tensor_copy(mask4[:, i, :], mtmp[:, 2, :]))
            for i, strict in enumerate((1, 0, 1, 0)):
                select(mask4[:, i, :], [[1, 128]], -strict, -1, 0.0)
            for i, strict in enumerate((1, 0, 1, 0)):
                block_ones(mask4s[:, i, :], 64, 64, 8)
                select(mask4s[:, i, :], [[1, 64]], -strict, -1, 0.0)
            block_ones(masks[:, :], 64, 64, 8)
            select(masks[:, :], [[-1, 64]], -1, 1, 0.0)
            link(pool.memset(selr[:, :, :], 0.0))
            select(selr[:, :, :], [[-1, MLH], [0, 128]], 0, 1, 1.0, ALU.not_equal)
            link(pool.memset(rst_m[:, :], 1.0))
            link(pool.memset(rst_m[:, 0:SEQ:MCH], 0.0))
            link(pool.memset(rst_m[:, SEQ:NT:NS], 0.0))
            link(pool.memset(rst_r[:, :], 1.0))
            link(pool.memset(rst_r[:, 0:SEQ:RCH], 0.0))
            pool.memset(rst_r[:, SEQ:NT:NS], 0.0).then_inc(s_const, 1)
            pool.wait_ge(S("mix_ready"), 8)
            pool.iota(io16[:, :], pattern=[[1, 16]], base=0, channel_multiplier=0,
                      allow_small_or_imprecise_dtypes=True).then_inc(S("iota_ready"), 1)
            pool.wait_ge(S("gather_start"), 1)
            for t, (t0, n) in enumerate(TILES):
                with pool.Fori(0, HEADS // 2) as i:
                    for hh in range(2):
                        g0 = 128 * t + 16 * hh
                        pool.wait_ge(S("u_used"), i * 32 + (LEAD + g0 - 16))
                        pool.wait_ge(S("v_used"), i * 32 + (LEAD + g0 - 16))
                        pool.tensor_copy(ucol[0:n, hh, :], idx[0:n, t, bass.ds(i * 32 + 16 * hh, 16)]
                                         ).then_inc(S("index_ready"), 1)
                        pool.wait_ge(S("index_ready"), i * 2 + (8 * t + hh + 1))
                        for ring, table, loaded, used in ((ub, pu, "u_loaded", "u_used"), (vb, pv, "v_loaded", "v_used")):
                            for j in range(16):
                                pool.wait_ge(S(used), i * 32 + (LEAD + g0 + j - RING + 1))
                                pool.sem_inc(S("u_slot_seen"), 1)
                                pool.indirect_dma_start(
                                    out=ring[0:n, j % RING, :], out_offset=None, in_=table,
                                    in_offset=bass.IndirectOffsetOnAxis(ap=ucol[0:n, hh, j:j + 1], axis=0)
                                ).then_inc(S(f"{loaded}{j % RING}"), 16)

        def loaded_count(i, g0, j):
            return i * (16 * 32 // RING) + 16 * ((g0 + j) // RING + 1)

        @block.scalar
        def _(act):
            k = [0]

            def link(ins):
                k[0] += 1
                ins.then_inc(c_act, 1)
                act.wait_ge(c_act, k[0])

            raised = {}

            def own(signal):
                raised[signal.name] = raised.get(signal.name, 0) + 1
                act.wait_ge(signal, raised[signal.name])

            act.wait_ge(s_x, 16)
            act.wait_ge(s_const, 1)
            for kt in range(KD):
                if kt >= 2:
                    act.wait_ge(s_sqf, kt - 1)
                act.activation(sq[:, kt % 2, :], xnT[:, kt, :], ACT.Square).then_inc(s_sq, 1)
                own(s_sq)
            act.wait_ge(s_sqf, KD)
            for dst, b in zip(main_samp(rb), (0, 1)):
                act.activation(dst, bank[b][:, 0:dst.shape[1]], ACT.Sqrt, bias=eps_t[:, 0:1], scale=1.0 / D
                               ).then_inc(s_sd, 1)
                own(s_sd)
            act.wait_ge(s_init, 16 * 8)
            for ji, (kind, p, c0, w, d) in enumerate(JOBS):
                b = 2 * (ji % 2)
                act.wait_ge(s_pj, ji + 1)
                if kind == "v":
                    n = TILES[d][1]
                    act.activation(vaug[0:n, d, :, 0:128], bank[b][0:n, :].rearrange("p (h e) -> p h e", h=MLH),
                                   ACT.Copy).then_inc(s_pe, 1)
                    own(s_pe)
                    continue
                if kind in "if":
                    dst = gi if kind == "i" else gf
                    bias = small[:, 0:1] if kind == "i" else small[:, 1:2]
                    act.activation(dst[:, 0:SEQ], bank[b][0:4, :], ACT.Identity, bias=bias)
                    act.activation(dst[:, SEQ:NT], bank[b + 1][0:4, 0:SAMP], ACT.Identity, bias=bias).then_inc(s_pe, 1)
                    own(s_pe)
                    continue
                if kind == "o":
                    act.activation(osig[:, d, 0:SEQ], bank[b][:, :], ACT.Sigmoid)
                    act.activation(osig[:, d, SEQ:NT], bank[b + 1][:, 0:SAMP], ACT.Sigmoid).then_inc(s_pe, 1)
                    own(s_pe)
                    continue
                ext, lead = (ext_q, 3) if kind == "q" else (ext_r, 1)
                act.activation(ext[:, d, lead:lead + SEQ], bank[b][:, :], ACT.Copy)
                act.activation(ext[:, d, lead + SEQ:].rearrange("p (b s) -> p b s", b=NB)[:, :, lead:],
                               bank[b + 1][:, 0:SAMP].rearrange("p (b s) -> p b s", b=NB), ACT.Copy).then_inc(s_pe, 1)
                own(s_pe)
            act.wait_ge(S("gate_abs"), 1)
            link(act.activation(rows["l"][:, :], rows["l"][:, :], ACT.Exp, scale=-1.0))
            act.activation(rows["l"][:, :], rows["l"][:, :], ACT.Ln, bias=eps_t[0:4, 2:3]).then_inc(S("gate_log"), 1)
            own(S("gate_log"))
            act.wait_ge(S("rows_ready"), 1)
            act.activation(rows["E2"][:, :], rows["E2"][:, :], ACT.Exp)
            act.activation(rows["flo"][:, :], rows["m"][:, :], ACT.Exp, scale=-1.0)
            act.activation(rows["W"][:, :], rows["W"][:, :], ACT.Exp).then_inc(S("rows_exp"), 1)
            own(S("rows_exp"))
            for h in range(MLH):
                for i in range(3):
                    act.wait_ge(S("bcast_done"), 3 * h + i + 1)
                    b = 2 * (i % 2)
                    act.activation(bc[:, i, 0:SEQ], bank[b][:, :], ACT.Copy)
                    act.activation(bc[:, i, SEQ:NT], bank[b + 1][:, 0:SAMP], ACT.Copy).then_inc(S("bcast_copied"), 1)
                    own(S("bcast_copied"))
                for i in range(2):
                    act.wait_ge(S("conv_ready"), 2 * h + i + 1)
                    act.activation(sg[:, i, :], pre[:, i, :], ACT.Sigmoid).then_inc(S("conv_sig"), 1)
                    own(S("conv_sig"))
                act.wait_ge(S("ktok_done"), h + 1)
                act.activation(ktok[:, 0:PT, :], bank[4][:, :].rearrange("p (t d) -> p t d", t=PT), ACT.Copy)
                act.activation(ktok[0:SAMP, PT, :], bank[5][0:SAMP, 0:128], ACT.Copy).then_inc(S("ktok_ready"), 1)
                own(S("ktok_ready"))
                act.wait_ge(S("dlog_ready"), h + 1)
                act.activation(dmat[:, 0:PT, :], dmat[:, 0:PT, :], ACT.Exp)
                act.activation(dmat[0:SAMP, PT, 0:SAMP], dmat[0:SAMP, PT, 0:SAMP], ACT.Exp).then_inc(S("d_ready"), 1)
                own(S("d_ready"))
                act.wait_ge(S("var_done"), h + 1)
                act.activation(hr[:, 0:SEQ], bank[2][:, :], ACT.Sqrt, bias=eps_t[:, 0:1], scale=1.0 / 128)
                act.activation(hr[:, SEQ:NT], bank[3][:, 0:SAMP], ACT.Sqrt, bias=eps_t[:, 0:1], scale=1.0 / 128
                               ).then_inc(S("std_ready"), 1)
                own(S("std_ready"))
            act.wait_ge(S("lora_in"), 1)
            act.activation(xwa[0:64, :], xwa[0:64, :], ACT.Tanh)
            act.activation(xg[:, :], xg[:, :], ACT.Sigmoid).then_inc(S("lora_act"), 1)
            own(S("lora_act"))
            c_tok = c_stg = c_nv = c_mg = c_ts = c_y0 = 0
            for p in range(4):
                act.wait_ge(S("lora_done"), p + 1)
                for b, name, fn, bias in ((0, "sw", ACT.Sigmoid, "w0"), (2, "av", ACT.Sigmoid, "a0"), (4, "gv", ACT.Copy, None)):
                    for dst, src in zip(main_samp(X[name]), (bank[b][:, :], bank[b + 1][:, 0:SAMP])):
                        if bias:
                            ins = act.activation(dst, src, fn, bias=pcol(bias, p))
                        else:
                            ins = act.activation(dst, src, fn)
                ins.then_inc(S("lora_out"), 1)
                own(S("lora_out"))
                act.wait_ge(S("kk_clamped"), p + 1)
                act.activation(X["t"][:, :], X["t"][:, :], ACT.Sqrt).then_inc(S("kk_norm"), 1)
                own(S("kk_norm"))
                act.wait_ge(S("cum_ready"), p + 1)
                act.activation(X["Ep"][:, :], X["cum"][:, :], ACT.Exp)
                act.activation(X["En"][:, :], X["cum"][:, :], ACT.Exp, scale=-1.0)
                act.activation(X["cm"][:, :], X["cm"][:, :], ACT.Exp).then_inc(S("decay_ready"), 1)
                own(S("decay_ready"))
                for g, tiles in enumerate(GROUPS):
                    us = units(g)
                    n = TILES[tiles[0]][1]
                    for li, t in enumerate(tiles):
                        c_tok += 1
                        act.wait_ge(S("tok_done"), c_tok)
                        act.activation(tok4[0:n, li, :, :], bank[4 * li + 3][0:n, :].rearrange("p (a d) -> p a d", a=4),
                                       ACT.Copy).then_inc(S("tok_ready"), 1)
                        own(S("tok_ready"))
                    nst = 4 if n == 128 else 3
                    for u in range(len(us)):
                        c_nv += 1
                        act.wait_ge(S("nv_done"), c_nv)
                        act.activation(NV[u][0:n, :], bank[2 * u + 1][0:n, 0:64], ACT.Copy).then_inc(S("nv_ready"), 1)
                        own(S("nv_ready"))
                    for s in range(nst - 1):
                        for u in range(len(us)):
                            act.wait_ge(S("stage_done"), (c_stg := c_stg + 1))
                            act.activation(XM[u][s % 2][0:n, 0:2, 0:n],
                                           bank[2 * u][0:n, 0:2 * n].rearrange("p (a d) -> p a d", a=2),
                                           ACT.Copy).then_inc(S("powers_ready"), 1)
                            own(S("powers_ready"))
                    c_stg += len(us)
                    if n == 128:
                        for m in range(2):
                            for u in range(len(us)):
                                c_mg += 1
                                act.wait_ge(S("merge_a"), c_mg)
                                act.activation(TB[u][:, :, :], bank[2 * u][:, 0:256].rearrange("p (a d) -> p a d", a=2),
                                               ACT.Copy).then_inc(S("merge_b"), 1)
                                own(S("merge_b"))
                    for u in range(len(us)):
                        c_ts += 1
                        act.wait_ge(S("ts_done"), c_ts)
                        act.activation(TS[u][0:n, :], bank[2 * u][0:n, 0:128], ACT.Copy).then_inc(S("ts_ready"), 1)
                        own(S("ts_ready"))
                    for li, t in enumerate(tiles):
                        c_y0 += 1
                        act.wait_ge(S("gh_done"), c_y0)
                        t0 = TILES[t][0]
                        act.activation(X["y"][:, t0:t0 + n], bank[4 * li][:, 128:128 + n], ACT.Copy).then_inc(S("y0_ready"), 1)
                        own(S("y0_ready"))
                act.wait_ge(S("gvar_done"), p + 1)
                act.activation(X["d"][:, 0:SEQ], bank[7][:, :], ACT.Sqrt, bias=eps_t[:, 1:2], scale=1.0 / 64)
                act.activation(X["d"][:, SEQ:NT], bank[0][:, 0:SAMP], ACT.Sqrt, bias=eps_t[:, 1:2], scale=1.0 / 64
                               ).then_inc(S("gstd_ready"), 1)
                own(S("gstd_ready"))
            for t, (t0, n) in enumerate(TILES):
                act.wait_ge(S("x1_ready"), 6 + t)
                link(act.activation(sc[0:n, 0:D], x1[0:n, t, :], ACT.Square, accum_out=st[0:n, t, 0:1]))
                act.activation(st[0:n, t, 1:2], st[0:n, t, 0:1], ACT.Sqrt, bias=eps_t[0:n, 0:1], scale=1.0 / D
                               ).then_inc(S("frms_ready"), 1)
                own(S("frms_ready"))
            for t, (t0, n) in enumerate(TILES):
                act.wait_ge(S("xfT_done"), t + 1)
                for half in range(2):
                    ins = act.activation(xfT[:, 4 * half:4 * half + 4, t0:t0 + n],
                                         bank[4 + 2 * (t % 2) + half][:, 0:4 * n].rearrange("p (k n) -> p k n", k=4), ACT.Copy)
                ins.then_inc(S("xfT_ready"), 1)
                own(S("xfT_ready"))
            for j in range(16):
                act.wait_ge(S("qproj_done"), j + 1)
                b = 2 * (j % 2)
                act.activation(qT[:, j, 0:SEQ], bank[b][:, :], ACT.Copy)
                act.activation(qT[:, j, SEQ:NT], bank[b + 1][:, 0:SAMP], ACT.Copy).then_inc(S("qT_ready"), 1)
                own(S("qT_ready"))
            for t, (t0, n) in enumerate(TILES):
                act.wait_ge(S("scores_done"), t + 1)
                if t:
                    act.wait_ge(S("routed"), t)
                for b in range(4):
                    ins = act.activation(sc[0:n, 512 * b:512 * b + 512], bank[4 + b][0:n, :], ACT.Copy)
                ins.then_inc(S("scores_ready"), 1)
                own(S("scores_ready"))
                act.wait_ge(S("shifted"), t + 1)
                act.activation(gate[0:n, t, :], gate[0:n, t, :], ACT.Exp).then_inc(S("gexp_ready"), 1)
                own(S("gexp_ready"))
            for t, (t0, n) in enumerate(TILES):
                with act.Fori(0, HEADS // 2) as i:
                    for hh in range(2):
                        g0 = 128 * t + 16 * hh
                        act.wait_ge(S("u_used"), i * 32 + (LEAD + g0 + 16))
                        act.activation(gel[0:n, hh, :], dots[0:n, hh, :], ACT.Gelu).then_inc(S("gelu_ready"), 1)
                        act.wait_ge(S("weight_ready"), i * 2 + (8 * t + hh + 1))
                        for j in range(16):
                            act.wait_ge(S("v_used"), i * 32 + (LEAD + g0 + j - 15))
                            act.activation(diag[0:n, j, 0:n], ident[0:n, 0:n], ACT.Copy, scale=wts[0:n, hh, j:j + 1]
                                           ).then_inc(S("diag_ready"), 1)
                act.wait_ge(S("x2_ready"), t + 1)
                link(act.activation(junk[0:n, :], x1[0:n, t, :], ACT.Square, accum_out=st[0:n, t, 2:3]))
                act.activation(st[0:n, t, 3:4], st[0:n, t, 2:3], ACT.Sqrt, bias=eps_t[0:n, 0:1], scale=1.0 / D
                               ).then_inc(S("yrms_ready"), 1)
                own(S("yrms_ready"))

        @block.tensor
        def _(pe):
            mm = pe.matmul
            pe.wait_ge(s_const, 1)
            for kt in range(KD):
                pe.wait_ge(s_sq, kt + 1)
                mm(bank[0][:, :], ones[:, :], sq[:, kt % 2, 0:SEQ], start=kt == 0, stop=kt == KD - 1)
                mm(bank[1][:, 0:SAMP], ones[:, :], sq[:, kt % 2, SEQ:NT], start=kt == 0, stop=kt == KD - 1
                   ).then_inc(s_sqf, 1)
            pe.wait_ge(s_xn, KD)
            for ji, (kind, p, c0, w, d) in enumerate(JOBS):
                b = 2 * (ji % 2)
                pe.wait_ge(s_w[p % 2], 16 * (p // 2 + 1))
                if ji >= 2:
                    pe.wait_ge(s_pe, ji - 1)
                wp = wbuf[p % 2]
                if kind == "v":
                    t0, n = TILES[d]
                    for kt in range(KD):
                        ins = mm(bank[b][0:n, :], xnT[:, kt, t0:t0 + n], wp[:, kt, 0:w], start=kt == 0, stop=kt == KD - 1)
                else:
                    for kt in range(KD):
                        mm(bank[b][0:w, :], wp[:, kt, c0:c0 + w], xnT[:, kt, 0:SEQ], start=kt == 0, stop=kt == KD - 1)
                        ins = mm(bank[b + 1][0:w, 0:SAMP], wp[:, kt, c0:c0 + w], xnT[:, kt, SEQ:NT],
                                 start=kt == 0, stop=kt == KD - 1)
                ins.then_inc(s_pj, 1)

            def both(b, lhsT, rhs, name):
                b, b2 = b
                mm(bank[b][:, :], lhsT, rhs[:, 0:SEQ], start=True, stop=True)
                mm(bank[b2][:, 0:SAMP], lhsT, rhs[:, SEQ:NT], start=True, stop=True).then_inc(S(name), 1)

            pe.wait_ge(s_const, 2)
            pe.wait_ge(s_pe, NJ)
            pe.wait_ge(S("rows_ready"), 1)
            pe.wait_ge(S("rows_exp"), 1)
            for t, (t0, n) in enumerate(TILES):
                for i, name in enumerate(("Ks", "W")):
                    ins = pe.transpose(bank[4][0:n, 8 * t + 4 * i:8 * t + 4 * i + 4], rows[name][:, t0:t0 + n],
                                       ident[0:4, 0:4])
            ins.then_inc(S("mcol_done"), 1)
            for h in range(MLH):
                if h:
                    pe.wait_ge(S("mix_ready"), h)
                for i, name in enumerate(("E1", "E2", "flo")):
                    if i >= 2:
                        pe.wait_ge(S("bcast_copied"), 3 * h + i - 1)
                    both((2 * (i % 2), 2 * (i % 2) + 1), selr[:, h, :], rows[name], "bcast_done")
                pe.wait_ge(S("qk_ready"), h + 1)
                pe.wait_ge(S("mcol_ready"), 1)
                for t, (t0, n) in enumerate(TILES):
                    dst = bank[4][:, 128 * t:128 * t + 128] if t < PT else bank[5][0:n, 0:128]
                    ins = pe.transpose(dst, kh[:, t0:t0 + n], ident[:, :])
                ins.then_inc(S("ktok_done"), 1)
                for t, (t0, n) in enumerate(TILES):
                    dst = bank[6][:, 128 * t:128 * t + 128] if t < PT else bank[7][0:n, 0:n]
                    ins = mm(dst, kh[:, t0:t0 + n], qh[:, t0:t0 + n], start=True, stop=True)
                ins.then_inc(S("qk_done"), 1)
                pe.wait_ge(S("wv_ready"), h + 1)
                pe.wait_ge(S("ktok_ready"), h + 1)
                pe.wait_ge(S("bcast_copied"), 3 * h + 3)
                for c in range(PT):
                    mm(bank[c // 2][:, 129 * (c % 2):129 * (c % 2) + 129], ktok[:, c, :], wv[:, c, :], start=True, stop=True)
                for b in range(NB):
                    ins = mm(bank[2 + b // 3][:, 129 * (b % 3):129 * (b % 3) + 129], ktok[0:SAMP, PT, :], wvX[:, b, :],
                             start=True, stop=True)
                ins.then_inc(S("upd_done"), 1)
                pe.wait_ge(S("p_ready"), h + 1)
                pe.wait_ge(S("qn_ready"), h + 1)
                for c in range(PT):
                    cs = slice(128 * c, 128 * c + 128)
                    mm(bank[6][:, cs], vaug[:, c, h, 0:128], pmat[:, c, :], start=True, stop=c == 0)
                    if c:
                        mm(bank[6][:, cs], cn[:, c - 1, 0:128], qs[:, cs], start=False, stop=True)
                    mm(bank[7][:, cs], ones[:, :], pmat[:, c, :], start=True, stop=c == 0)
                    if c:
                        mm(bank[7][:, cs], ones[:, :], qn[:, cs], start=False, stop=True)
                mm(bank[5][:, 0:SAMP], vaug[0:SAMP, PT, h, 0:128], pmat[0:SAMP, PT, 0:SAMP], start=True, stop=False,
                   skip_group_check=True)
                for b in range(NB):
                    mm(bank[5][:, 8 * b:8 * b + 8], cn0[:, b, h, 0:128], qs[:, SEQ + 8 * b:SEQ + 8 * b + 8],
                       start=False, stop=True, skip_group_check=True)
                mm(bank[5][:, 64:128], ones[0:SAMP, :], pmat[0:SAMP, PT, 0:SAMP], start=True, stop=False)
                mm(bank[5][:, 64:128], ones[:, :], qn[:, SEQ:NT], start=False, stop=True).then_inc(S("num_done"), 1)
                pe.wait_ge(S("h_ready"), h + 1)
                both((0, 1), ones[:, :], hb, "mean_done")
                pe.wait_ge(S("hsq_ready"), h + 1)
                both((2, 3), ones[:, :], hq, "var_done")
            c_tok = c_u = c_t = c_nv = c_stg = c_pw = c_mg = c_md = c_ts = c_gh = c_st = 0
            for p in range(4):
                pc = slice(128 * p, 128 * p + 128)
                pe.wait_ge(S("lora_act"), 1)
                pe.wait_ge(S("mix_ready"), 4 + p)
                for b, (lhsT, rhs) in enumerate(((w2[:, pc], xwa[0:64, :]), (a2[64:128, pc], xwa[64:128, :]), (g2[:, pc], xg))):
                    mm(bank[2 * b][:, :], lhsT, rhs[:, 0:SEQ], start=True, stop=True)
                    ins = mm(bank[2 * b + 1][:, 0:SAMP], lhsT, rhs[:, SEQ:NT], start=True, stop=True)
                ins.then_inc(S("lora_done"), 1)
                pe.wait_ge(S("kk_squares"), p + 1)
                both((6, 7), blk[:, :], X["t"], "kk_summed")
                pe.wait_ge(S("chan_ready"), p + 1)
                both((0, 1), blk[:, :], X["t"], "bonus_done")
                pe.wait_ge(S("bonus_ready"), p + 1)
                for g, tiles in enumerate(GROUPS):
                    us = units(g)
                    n = TILES[tiles[0]][1]
                    if p or g:
                        pe.wait_ge(S("gh_copied"), c_gh)
                        pe.wait_ge(S("y0_ready"), c_gh)
                    for li, t in enumerate(tiles):
                        t0 = TILES[t][0]
                        for a, src in enumerate((AR[:, 0, :], X["be"], X["ka"], X["v"])):
                            ins = pe.transpose(bank[4 * li + 3][0:n, 128 * a:128 * a + 128], src[:, t0:t0 + n], ident[:, :])
                        ins.then_inc(S("tok_done"), 1)
                    for u, (t, h) in enumerate(us):
                        t0 = TILES[t][0]
                        hs, ts_ = slice(64 * h, 64 * h + 64), slice(t0, t0 + n)
                        for a, key in enumerate((X["be"], X["ka"])):
                            ins = mm(bank[2 * u][0:n, 2 * a * n:2 * (a + 1) * n], key[hs, ts_], AR[hs, :, ts_],
                                     start=True, stop=True)
                        ins.then_inc(S("gram_done"), 1)
                    c_tok += len(tiles)
                    pe.wait_ge(S("tok_ready"), c_tok)
                    for u, (t, h) in enumerate(us):
                        t0 = TILES[t][0]
                        hs, ts_ = slice(64 * h, 64 * h + 64), slice(t0, t0 + n)
                        mm(bank[2 * u + 1][0:n, 0:n], AR[hs, 0, ts_], X["be"][hs, ts_], start=True, stop=True
                           ).then_inc(S("m_done"), 1)
                    for u, (t, h) in enumerate(us):
                        pe.wait_ge(S("masked"), (c_u := c_u + 1))
                        mm(bank[2 * u + 1][0:n, 0:64], G4[u][0:n, 2, 0:n], tok4[0:n, u // 2, 3, 64 * h:64 * h + 64],
                           start=True, stop=True).then_inc(S("nv_done"), 1)
                    nst = 4 if n == 128 else 3
                    for s in range(nst):
                        for u in range(len(us)):
                            if s == 0:
                                M, MT = M3[u][0:n, 0, 0:n], G4[u][0:n, 0, 0:n]
                                mm(bank[2 * u][0:n, 0:n], MT, M, start=True, stop=True)
                                ins = mm(bank[2 * u][0:n, n:2 * n], M, MT, start=True, stop=True)
                            else:
                                c_pw += 1
                                pe.wait_ge(S("powers_ready"), c_pw)
                                pe.wait_ge(S("inverse_step"), c_stg - len(us) + 1)
                                old = XM[u][(s - 1) % 2]
                                if s < nst - 1:
                                    mm(bank[2 * u][0:n, 0:n], old[0:n, 1, 0:n], old[0:n, 0, 0:n], start=True, stop=True)
                                    ins = mm(bank[2 * u][0:n, n:3 * n], old[0:n, 0, 0:n], old[0:n, 1:3, 0:n],
                                             start=True, stop=True)
                                else:
                                    ins = mm(bank[2 * u][0:n, 2 * n:3 * n], old[0:n, 0, 0:n], old[0:n, 2, 0:n],
                                             start=True, stop=True)
                            ins.then_inc(S("stage_done"), 1)
                            c_stg += 1
                    c_md_step = c_stg - len(us)
                    R = [XM[u][(nst - 1) % 2] for u in range(len(us))]
                    if n == 128:
                        for m in range(2):
                            for u in range(len(us)):
                                if m == 0:
                                    pe.wait_ge(S("inverse_step"), c_stg - len(us) + u + 1)
                                else:
                                    pe.wait_ge(S("merged"), c_md - len(us) + u + 1)
                                r = XM[u][(nst - 1 + m) % 2][:, 2, :]
                                pe.transpose(bank[2 * u][:, 0:128], r, ident[:, :])
                                mm(bank[2 * u][:, 128:256], M3[u][:, 1 + m, :], r, start=True, stop=True
                                   ).then_inc(S("merge_a"), 1)
                            for u in range(len(us)):
                                c_mg += 1
                                pe.wait_ge(S("merge_b"), c_mg)
                                if m == 0:
                                    pe.wait_ge(S("nv_ready"), c_nv + u + 1)
                                mm(bank[2 * u + 1][:, 0:128], TB[u][:, 0, :], TB[u][:, 1, :], start=True, stop=True
                                   ).then_inc(S("merge_c"), 1)
                                c_md += 1
                        R = [XM[u][(nst + 1) % 2] for u in range(len(us))]
                    for u, (t, h) in enumerate(us):
                        if n == 128:
                            pe.wait_ge(S("merged"), c_md - len(us) + u + 1)
                        else:
                            pe.wait_ge(S("inverse_step"), c_stg - len(us) + u + 1)
                        pe.wait_ge(S("nv_ready"), c_nv + u + 1)
                        mm(bank[2 * u][0:n, 0:64], R[u][0:n, 2, 0:n], tok4[0:n, u // 2, 0, 64 * h:64 * h + 64],
                           start=True, stop=True)
                        mm(bank[2 * u][0:n, 64:128], R[u][0:n, 2, 0:n], NV[u][0:n, :], start=True, stop=True
                           ).then_inc(S("ts_done"), 1)
                    c_nv += len(us)
                    if n < 128:
                        pe.wait_ge(S("spread"), p + 1)
                    for li, t in enumerate(tiles):
                        for h in range(2):
                            u = 2 * li + h
                            c_ts += 1
                            pe.wait_ge(S("ts_ready"), c_ts)
                        for h in range(2):
                            u = 2 * li + h
                            hs = slice(64 * h, 64 * h + 64)
                            ta, sa = TS[u][0:n, 0:64], TS[u][0:n, 64:128]
                            tk = tok4[0:n, li, :, hs]
                            ru, rv, rw = bank[4 * li], bank[4 * li + 1], bank[4 * li + 3]
                            mm(ru[hs, 0:n], ta, G4[u][0:n, 1, 0:n], start=True, stop=True)
                            mm(ru[hs, 128:128 + n], sa, G4[u][0:n, 1, 0:n], start=True, stop=False)
                            mm(ru[hs, 128:128 + n], tk[:, 3, :], G4[u][0:n, 3, 0:n], start=False, stop=True)
                            if n == 128:
                                for c in range(2):
                                    cs, dst = slice(64 * c, 64 * c + 64), (rv, rw)[c]
                                    mm(dst[hs, 0:64], ta[cs, :], tk[cs, 1, :], start=True, stop=True)
                                    mm(dst[hs, 64:128], tk[cs, 1, :], sa[cs, :], start=True, stop=False)
                                    ins = mm(dst[hs, 64:128], tk[cs, 2, :], tk[cs, 3, :], start=False, stop=True)
                            else:
                                mm(rv[hs, :], ta, bX[:, :, hs], start=True, stop=True)
                                for c in range(NB):
                                    mm(rw[hs, 64 * c:64 * c + 64], bX[:, c, hs], sa, start=True, stop=False)
                                    ins = mm(rw[hs, 64 * c:64 * c + 64], kX[:, c, hs], tk[:, 3, :], start=False, stop=True)
                        ins.then_inc(S("gh_done"), 1)
                        c_gh += 1
                pe.wait_ge(S("gh_copied"), c_gh)
                pe.wait_ge(S("y0_ready"), c_gh)
                for b in range(NB):
                    for h in range(2):
                        hs = slice(64 * h, 64 * h + 64)
                        ins = mm(bank[2][hs, 64 * b:64 * b + 64], GtS[hs, b, :], s0[hs, b, p, :], start=True, stop=True)
                ins.then_inc(S("sstep_done"), 1)
                for c in range(1, 8):
                    c_st += 1
                    pe.wait_ge(S("state_ready"), c_st + p)
                    for h in range(2):
                        hs = slice(64 * h, 64 * h + 64)
                        ins = mm(bank[c % 2][hs, 0:64], Gt[hs, c, :], Sst[hs, c - 1, :], start=True, stop=True)
                    ins.then_inc(S("state_step"), 1)
                for c in range(1, 8):
                    for h in range(2):
                        hs = slice(64 * h, 64 * h + 64)
                        cs = slice(64 * c, 64 * c + 64)
                        mm(bank[3][hs, cs], Sst[hs, c - 1, :], X["reff"][hs, cs], start=True, stop=True)
                for b in range(NB):
                    for h in range(2):
                        hs = slice(64 * h, 64 * h + 64)
                        ins = mm(bank[4][hs, 8 * b:8 * b + 8], s0[hs, b, p, :], X["reff"][hs, SEQ + 8 * b:SEQ + 8 * b + 8],
                                 start=True, stop=True)
                ins.then_inc(S("y_inter"), 1)
                pe.wait_ge(S("y_full"), p + 1)
                both((5, 6), blk[:, :], X["y"], "gmean_done")
                pe.wait_ge(S("gsq_ready"), p + 1)
                both((7, 0), blk[:, :], X["kk"], "gvar_done")
            pe.wait_ge(S("mix_ready"), 8)
            for half in range(2):
                pe.wait_ge(s_wo, 16 * (half + 1))
                for t, (t0, n) in enumerate(TILES):
                    jj = 5 * half + t
                    if jj >= 4:
                        pe.wait_ge(S("x1_ready"), jj - 3)
                    for kt in range(KD):
                        ins = mm(bank[jj % 4][0:n, :], mixT[:, kt, t0:t0 + n], wo[:, kt, :], start=kt == 0, stop=kt == KD - 1)
                    ins.then_inc(S("outproj_done"), 1)
            for t, (t0, n) in enumerate(TILES):
                pe.wait_ge(S("xf_ready"), t + 1)
                if t >= 2:
                    pe.wait_ge(S("xfT_ready"), t - 1)
                for kt in range(KD):
                    ins = pe.transpose(bank[4 + 2 * (t % 2) + kt // 4][:, n * (kt % 4):n * (kt % 4) + n],
                                       xf[0:n, t, 128 * kt:128 * kt + 128], ident[0:n, 0:n])
                ins.then_inc(S("xfT_done"), 1)
            pe.wait_ge(S("xfT_ready"), 5)
            pe.wait_ge(S("x1_ready"), 10)
            for j in range(16):
                pp = j // 4
                pe.wait_ge(s_wq[pp % 2], 16 * (pp // 2 + 1))
                if j >= 2:
                    pe.wait_ge(S("qT_ready"), j - 1)
                b = 2 * (j % 2)
                for kt in range(KD):
                    lhsT = wq[pp % 2][:, kt, 128 * (j % 4):128 * (j % 4) + 128]
                    mm(bank[b][:, :], lhsT, xfT[:, kt, 0:SEQ], start=kt == 0, stop=kt == KD - 1)
                    ins = mm(bank[b + 1][:, 0:SAMP], lhsT, xfT[:, kt, SEQ:NT], start=kt == 0, stop=kt == KD - 1)
                ins.then_inc(S("qproj_done"), 1)
            pe.wait_ge(S("qT_ready"), 16)
            pe.wait_ge(s_sub, 16)
            for t, (t0, n) in enumerate(TILES):
                if t:
                    pe.wait_ge(S("scores_ready"), t)
                for j in range(16):
                    ins = mm(bank[4 + j // 4][0:n, 128 * (j % 4):128 * (j % 4) + 128], qT[:, j, t0:t0 + n], subT[:, j, :],
                             start=True, stop=True)
                ins.then_inc(S("scores_done"), 1)
            pe.wait_ge(S("zeros_ready"), 1)
            for t, (t0, n) in enumerate(TILES):
                acc = [bank[2 * (t % 2)], bank[2 * (t % 2) + 1]]
                if t >= 2:
                    pe.wait_ge(S("x2_ready"), t - 1)
                for half in range(2):
                    mm(acc[half][0:n, :], zer[0:n, 0:n], zer[0:n, :], start=True, stop=False, skip_group_check=True)
                with pe.Fori(0, HEADS // 2) as i:
                    for hh in range(2):
                        g0 = 128 * t + 16 * hh
                        for j in range(16):
                            pe.wait_ge(S("diag_ready"), i * 32 + (g0 + j + 1))
                            pe.wait_ge(S(f"v_loaded{j % RING}"), loaded_count(i, g0, j))
                            pe.sem_inc(S("v_slot_seen"), 1)
                            for half in range(2):
                                ins = mm(acc[half][0:n, :], diag[0:n, j, 0:n], vb[0:n, j % RING, 512 * half:512 * half + 512],
                                         start=False, stop=False, skip_group_check=True)
                            ins.then_inc(S("v_used"), 1)
                for half in range(2):
                    ins = mm(acc[half][0:n, :], zer[0:n, 0:n], zer[0:n, :], start=False, stop=True, skip_group_check=True)
                ins.then_inc(S("acc_done"), 1)

        @block.vector
        def _(dve):
            k = [0]

            def link(ins):
                k[0] += 1
                ins.then_inc(c_dve, 1)
                dve.wait_ge(c_dve, k[0])

            raised = {}

            def own(signal):
                raised[signal.name] = raised.get(signal.name, 0) + 1
                dve.wait_ge(signal, raised[signal.name])

            TT, TS_, STT = dve.tensor_tensor, dve.tensor_scalar, dve.scalar_tensor_tensor

            def seqs(ap, lead):
                return ap[:, lead + SEQ:].rearrange("p (b s) -> p b s", b=NB)

            def steps(ap):
                return ap.rearrange("p (b s) -> p b s", b=NB)

            dve.wait_ge(s_par, 16)
            dve.wait_ge(s_sd, 2)
            link(dve.reciprocal(rb[:, :], rb[:, :]))
            for kt in range(KD):
                STT(out=xnT[:, kt, :], in0=xnT[:, kt, :], scalar=pcol("g_mix", kt), in1=rb[:, :], op0=ALU.mult,
                    op1=ALU.mult).then_inc(s_xn, 1)
                own(s_xn)
            dve.wait_ge(s_init, 16 * 8)
            link(dve.tensor_copy(ext_q[:, :, 3 + SEQ:].rearrange("p c (b s) -> p c b s", b=NB)[:, :, :, 0:3], conv0[:, :, :, :]))
            link(dve.tensor_copy(ext_r[:, :, 1 + SEQ:].rearrange("p c (b s) -> p c b s", b=NB)[:, :, :, 0], shift0[:, :, :]))
            dve.wait_ge(s_const, 2)
            dve.wait_ge(s_pe, NJ)
            r = rows
            STT(out=r["l"][:, :], in0=gf[:, :], scalar=-1.0, in1=gf[:, :], op0=ALU.mult, op1=ALU.max).then_inc(S("gate_abs"), 1)
            own(S("gate_abs"))
            link(TS_(gf[:, :], gf[:, :], 0.0, None, ALU.min))
            dve.wait_ge(S("gate_log"), 1)
            link(TT(gf[:, :], gf[:, :], r["l"][:, :], ALU.subtract))
            link(dve.tensor_tensor_scan(r["b"][:, :], rst_m[:, :], gf[:, :], 0.0, ALU.mult, ALU.add))
            link(dve.tensor_tensor_scan(r["m"][:, 0:SEQ], gf[:, 0:SEQ], gi[:, 0:SEQ], NEG, ALU.add, ALU.max))
            for b in range(NB):
                s = slice(SEQ + NS * b, SEQ + NS * b + NS)
                link(dve.tensor_tensor_scan(r["m"][:, s], gf[:, s], gi[:, s], small[:, 2 + b:3 + b], ALU.add, ALU.max))
            link(TT(r["E1"][:, :], r["b"][:, :], r["m"][:, :], ALU.subtract))
            link(TT(r["Ks"][:, :], gi[:, :], r["b"][:, :], ALU.subtract))
            link(TS_(r["E2"][:, 0:MCH], r["E1"][:, 0:MCH], NEG, None, ALU.add))
            for c in range(1, PT):
                s = slice(MCH * c, MCH * c + MCH)
                link(TS_(r["E2"][:, s], r["E1"][:, s], r["m"][:, MCH * c - 1:MCH * c], None, ALU.add))
            for b in range(NB):
                s = slice(SEQ + NS * b, SEQ + NS * b + NS)
                link(TS_(r["E2"][:, s], r["E1"][:, s], small[:, 2 + b:3 + b], None, ALU.add))
            for lo, hi, w in ((0, SEQ, MCH), (SEQ, NT, NS)):
                v = [r[n][:, lo:hi].rearrange("p (c w) -> p c w", w=w) for n in ("W", "Ks", "E1")]
                last = TT(v[0], v[1], v[2][:, :, w - 1:w].to_broadcast([4, (hi - lo) // w, w]), ALU.add)
                if lo == 0:
                    link(last)
            last.then_inc(S("rows_ready"), 1)
            own(S("rows_ready"))
            link(dve.tensor_copy(mo[:, 0:1], r["m"][:, SEQ - 1:SEQ]))
            dve.tensor_copy(mo[:, 1:], r["m"][:, SEQ + NS - 1:NT:NS]).then_inc(S("m_ready"), 1)
            own(S("m_ready"))
            dve.wait_ge(S("mcol_done"), 1)
            link(dve.tensor_copy(mcol[:, 0:PT, :, :], bank[4][:, 0:8 * PT].rearrange("p (t a h) -> p t a h", t=PT, a=2)))
            link(dve.tensor_copy(mcol[0:SAMP, PT, :, :], bank[4][0:SAMP, 8 * PT:8 * PT + 8].rearrange("p (a h) -> p a h", a=2)))
            for h in range(MLH):
                last = TS_(wcolX[:, h, :], seqm[:, :], mcol[0:SAMP, PT, 1, h:h + 1], None, ALU.mult)
            last.then_inc(S("mcol_ready"), 1)
            own(S("mcol_ready"))
            dve.wait_ge(S("mcol_ready"), 1)
            for h in range(MLH):
                for i, ct in enumerate((h, 4 + h)):
                    for part in range(2):
                        for j in range(CW):
                            if part == 0:
                                src, dst = ext_q[:, ct, j:j + SEQ], pre[:, i, 0:SEQ]
                            else:
                                src, dst = seqs(ext_q[:, ct, :], 3)[:, :, j:j + NS], steps(pre[:, i, SEQ:NT])
                            w = pcol("conv_w", 8 * j + ct)
                            if j == 0:
                                link(TS_(dst, src, w, pcol("conv_b", ct), ALU.mult, ALU.add))
                            else:
                                last = STT(out=dst, in0=src, scalar=w, in1=dst, op0=ALU.mult, op1=ALU.add)
                                if part == 0 or j < CW - 1:
                                    link(last)
                    last.then_inc(S("conv_ready"), 1)
                    own(S("conv_ready"))
                dve.wait_ge(S("conv_sig"), 2 * h + 2)
                link(TT(qh[:, :], pre[:, 0, :], sg[:, 0, :], ALU.mult))
                STT(out=kh[:, :], in0=pre[:, 1, :], scalar=128 ** -0.5, in1=sg[:, 1, :], op0=ALU.mult, op1=ALU.mult
                    ).then_inc(S("qk_ready"), 1)
                own(S("qk_ready"))
                dve.wait_ge(S("bcast_copied"), 3 * h + 3)
                link(TT(qs[:, :], qh[:, :], bc[:, 1, :], ALU.mult))
                for t, (t0, n) in enumerate(TILES):
                    last = STT(out=dmat[0:n, t, 0:n], in0=bc[0:n, 0, t0:t0 + n], scalar=mcol[0:n, t, 0, h:h + 1],
                               in1=negm[:, :] if t < PT else negs[:, :], op0=ALU.add, op1=ALU.add)
                last.then_inc(S("dlog_ready"), 1)
                own(S("dlog_ready"))
                for c in range(PT):
                    TS_(wv[:, c, :], vaug[:, c, h, :], mcol[:, c, 1, h:h + 1], None, ALU.mult)
                for b in range(NB):
                    last = TS_(wvX[:, b, :], vaug[0:SAMP, PT, h, :], wcolX[:, h, b:b + 1], None, ALU.mult)
                last.then_inc(S("wv_ready"), 1)
                own(S("wv_ready"))
                dve.wait_ge(S("qk_done"), h + 1)
                dve.wait_ge(S("d_ready"), h + 1)
                link(TT(pmat[:, 0:PT, :], bank[6][:, :].rearrange("p (t n) -> p t n", t=PT), dmat[:, 0:PT, :], ALU.mult))
                TT(pmat[0:SAMP, PT, 0:SAMP], bank[7][0:SAMP, 0:SAMP], dmat[0:SAMP, PT, 0:SAMP], ALU.mult).then_inc(S("p_ready"), 1)
                own(S("p_ready"))
                dve.wait_ge(S("upd_done"), h + 1)
                if h:
                    dve.wait_ge(s_out, 16 * (1 + 2 * h))
                link(dve.tensor_copy(cn[:, 0, :], bank[0][:, 0:129]))
                for c in range(1, PT):
                    link(STT(out=cn[:, c, :], in0=cn[:, c - 1, :], scalar=bc[:, 1, MCH * (c + 1) - 1:MCH * (c + 1)],
                             in1=bank[c // 2][:, 129 * (c % 2):129 * (c % 2) + 129], op0=ALU.mult, op1=ALU.add))
                for b in range(NB):
                    e = SEQ + NS * (b + 1)
                    last = STT(out=cnS[:, b, :], in0=cn0[:, b, h, :], scalar=bc[:, 1, e - 1:e],
                               in1=bank[2 + b // 3][:, 129 * (b % 3):129 * (b % 3) + 129], op0=ALU.mult, op1=ALU.add)
                last.then_inc(S("cn_ready"), 1)
                own(S("cn_ready"))
                for c in range(1, PT):
                    s = slice(MCH * c, MCH * c + MCH)
                    TS_(qn[:, s], qs[:, s], cn[:, c - 1, 128:129], None, ALU.mult)
                TT(steps(qn[:, SEQ:NT]), steps(qs[:, SEQ:NT]), cn0[:, :, h, 128:129].to_broadcast([128, NB, NS]), ALU.mult
                   ).then_inc(S("qn_ready"), 1)
                own(S("qn_ready"))
                dve.wait_ge(S("num_done"), h + 1)
                for dst, den, fl in ((hr[:, 0:SEQ], bank[7][:, :], bc[:, 2, 0:SEQ]), (hr[:, SEQ:NT], bank[5][:, 64:128], bc[:, 2, SEQ:NT])):
                    link(STT(out=dst, in0=den, scalar=-1.0, in1=fl, op0=ALU.mult, op1=ALU.max))
                    link(TT(dst, den, dst, ALU.max))
                link(dve.reciprocal(hr[:, :], hr[:, :]))
                link(TT(hb[:, 0:SEQ], bank[6][:, :], hr[:, 0:SEQ], ALU.mult))
                TT(hb[:, SEQ:NT], bank[5][:, 0:SAMP], hr[:, SEQ:NT], ALU.mult).then_inc(S("h_ready"), 1)
                own(S("h_ready"))
                dve.wait_ge(S("mean_done"), h + 1)
                dve.wait_ge(S("h_ready"), h + 1)
                for dst, src in zip(main_samp(hb), (bank[0][:, :], bank[1][:, 0:SAMP])):
                    link(STT(out=dst, in0=src, scalar=-1.0 / 128, in1=dst, op0=ALU.mult, op1=ALU.add))
                TT(hq[:, :], hb[:, :], hb[:, :], ALU.mult).then_inc(S("hsq_ready"), 1)
                own(S("hsq_ready"))
                dve.wait_ge(S("std_ready"), h + 1)
                link(dve.reciprocal(hr[:, :], hr[:, :]))
                link(STT(out=hb[:, :], in0=hb[:, :], scalar=pcol("ml_g", h), in1=hr[:, :], op0=ALU.mult, op1=ALU.mult))
                TT(mixT[:, h, :], hb[:, :], osig[:, h, :], ALU.mult).then_inc(S("mix_ready"), 1)
                own(S("mix_ready"))
            eq = ext_q[:, :, 3 + SEQ:].rearrange("p c (b s) -> p c b s", b=NB)
            er = ext_r[:, :, 1 + SEQ:].rearrange("p c (b s) -> p c b s", b=NB)
            link(dve.tensor_copy(conv_t[:, :, 0, :], ext_q[:, :, SEQ:SEQ + 3]))
            dve.tensor_copy(conv_t[:, :, 1:, :], eq[:, :, :, NS:NS + 3]).then_inc(S("tails_ready"), 1)
            own(S("tails_ready"))
            link(dve.tensor_copy(shift_t[:, :, 0], ext_r[:, :, SEQ]))
            dve.tensor_copy(shift_t[:, :, 1:], er[:, :, :, NS]).then_inc(S("tails_ready"), 1)
            own(S("tails_ready"))
            dve.wait_ge(s_out, 16 * 11)
            dve.wait_ge(S("mix_ready"), 4)

            def shifted(dst, ct):
                for part in range(2):
                    if part == 0:
                        cur, prev = ext_r[:, ct, 1:1 + SEQ], ext_r[:, ct, 0:SEQ]
                        d, o = X["d"][:, 0:SEQ], dst[:, 0:SEQ]
                    else:
                        e = seqs(ext_r[:, ct, :], 1)
                        cur, prev = e[:, :, 1:], e[:, :, 0:NS]
                        d, o = steps(X["d"][:, SEQ:NT]), steps(dst[:, SEQ:NT])
                    link(TT(d, prev, cur, ALU.subtract))
                    last = STT(out=o, in0=d, scalar=pcol("mu", ct), in1=cur, op0=ALU.mult, op1=ALU.add)
                    if part == 0:
                        link(last)
                return last

            link(shifted(xwa, 12))
            shifted(xg, 13).then_inc(S("lora_in"), 1)
            own(S("lora_in"))
            c_u = c_stg = c_md = c_gh = c_st = c_tok = c_pw = 0
            for p in range(4):
                link(shifted(X["r"], p))
                link(shifted(X["k"], 4 + p))
                link(shifted(X["v"], 8 + p))
                link(TS_(X["kk"][:, :], X["k"][:, :], pcol("k_k", p), None, ALU.mult))
                TT(X["t"][:, :], X["kk"][:, :], X["kk"][:, :], ALU.mult).then_inc(S("kk_squares"), 1)
                own(S("kk_squares"))
                dve.wait_ge(S("kk_summed"), p + 1)
                for dst, src in zip(main_samp(X["t"]), (bank[6][:, :], bank[7][:, 0:SAMP])):
                    last = TS_(dst, src, 1e-24, None, ALU.max)
                last.then_inc(S("kk_clamped"), 1)
                own(S("kk_clamped"))
                dve.wait_ge(S("lora_out"), p + 1)
                link(TS_(X["sw"][:, :], X["sw"][:, :], -math.exp(-0.5), None, ALU.mult))
                link(dve.tensor_tensor_scan(X["cum"][:, :], rst_r[:, :], X["sw"][:, :], 0.0, ALU.mult, ALU.add))
                TT(X["cm"][:, :], X["cum"][:, :], X["sw"][:, :], ALU.subtract).then_inc(S("cum_ready"), 1)
                own(S("cum_ready"))
                dve.wait_ge(S("kk_norm"), p + 1)
                link(dve.reciprocal(X["t"][:, :], X["t"][:, :]))
                link(TT(X["kk"][:, :], X["kk"][:, :], X["t"][:, :], ALU.mult))
                link(TS_(X["t"][:, :], X["av"][:, :], 1.0, pcol("k_a", p), ALU.subtract, ALU.mult))
                link(STT(out=X["kf"][:, :], in0=X["t"][:, :], scalar=1.0, in1=X["k"][:, :], op0=ALU.add, op1=ALU.mult))
                link(TT(X["be"][:, :], X["kk"][:, :], X["av"][:, :], ALU.mult))
                dve.wait_ge(S("decay_ready"), p + 1)
                link(TT(X["be"][:, :], X["be"][:, :], X["En"][:, :], ALU.mult))
                link(STT(out=AR[:, 0, :], in0=X["kk"][:, :], scalar=-1.0, in1=X["cm"][:, :], op0=ALU.mult, op1=ALU.mult))
                link(TT(AR[:, 1, :], X["r"][:, :], X["Ep"][:, :], ALU.mult))
                link(TT(X["ka"][:, :], X["kf"][:, :], X["En"][:, :], ALU.mult))
                STT(out=X["t"][:, :], in0=X["r"][:, :], scalar=pcol("r_k", p), in1=X["kf"][:, :], op0=ALU.mult,
                    op1=ALU.mult).then_inc(S("chan_ready"), 1)
                own(S("chan_ready"))
                dve.wait_ge(S("bonus_done"), p + 1)
                for dst, src, v in zip(main_samp(X["bv"]), (bank[0][:, :], bank[1][:, 0:SAMP]), main_samp(X["v"])):
                    last = TT(dst, src, v, ALU.mult)
                last.then_inc(S("bonus_ready"), 1)
                own(S("bonus_ready"))
                for g, tiles in enumerate(GROUPS):
                    us = units(g)
                    n = TILES[tiles[0]][1]
                    m4, m3 = (mask4[:, :, :], mask3[:, :, :]) if n == 128 else (mask4s[:, :, :], masks[:, :])
                    for u in range(len(us)):
                        dve.wait_ge(S("gram_done"), c_u + u + 1)
                        link(TT(G4[u][0:n, :, 0:n], bank[2 * u][0:n, 0:4 * n].rearrange("p (a n) -> p a n", a=4), m4, ALU.mult))
                    for u in range(len(us)):
                        c_u += 1
                        dve.wait_ge(S("m_done"), c_u)
                        src = bank[2 * u + 1][0:n, 0:n]
                        if n == 128:
                            TT(M3[u][:, :, :], src.unsqueeze(1).to_broadcast([128, 3, 128]), m3, ALU.mult).then_inc(S("masked"), 1)
                            own(S("masked"))
                        else:
                            TT(M3[u][0:n, 0, 0:n], src, m3, ALU.mult).then_inc(S("masked"), 1)
                            own(S("masked"))
                    c_tok += len(tiles)
                    if n < 128:
                        dve.wait_ge(S("tok_ready"), c_tok)
                        link(TT(bX[:, :, :], tok4[0:n, 0, 1, :].unsqueeze(1).to_broadcast([n, NB, 128]),
                                seqm[:, :].unsqueeze(2).to_broadcast([n, NB, 128]), ALU.mult))
                        TT(kX[:, :, :], tok4[0:n, 0, 2, :].unsqueeze(1).to_broadcast([n, NB, 128]),
                           seqm[:, :].unsqueeze(2).to_broadcast([n, NB, 128]), ALU.mult).then_inc(S("spread"), 1)
                        own(S("spread"))
                    nst = 4 if n == 128 else 3
                    for s in range(nst):
                        for u in range(len(us)):
                            c_stg += 1
                            if s == 0:
                                TT(XM[u][0][0:n, 2, 0:n], G4[u][0:n, 0, 0:n], ident[0:n, 0:n], ALU.add
                                   ).then_inc(S("inverse_step"), 1)
                                own(S("inverse_step"))
                            else:
                                dve.wait_ge(S("stage_done"), c_stg)
                                dve.wait_ge(S("powers_ready"), c_pw + min(len(us) * s + u + 1, len(us) * (nst - 1)))
                                dve.wait_ge(S("inverse_step"), c_stg - len(us))
                                TT(XM[u][s % 2][0:n, 2, 0:n], bank[2 * u][0:n, 2 * n:3 * n], XM[u][(s - 1) % 2][0:n, 2, 0:n],
                                   ALU.add).then_inc(S("inverse_step"), 1)
                                own(S("inverse_step"))
                    c_pw += len(us) * (nst - 1)
                    if n == 128:
                        for m in range(2):
                            for u in range(len(us)):
                                c_md += 1
                                dve.wait_ge(S("merge_c"), c_md)
                                if m == 0:
                                    dve.wait_ge(S("inverse_step"), c_stg)
                                else:
                                    dve.wait_ge(S("merged"), c_md - len(us))
                                TT(XM[u][(nst + m) % 2][:, 2, :], bank[2 * u + 1][:, 0:128], XM[u][(nst - 1 + m) % 2][:, 2, :],
                                   ALU.add).then_inc(S("merged"), 1)
                                own(S("merged"))
                    for li, t in enumerate(tiles):
                        t0 = TILES[t][0]
                        c_gh += 1
                        dve.wait_ge(S("gh_done"), c_gh)
                        dve.wait_ge(S("y0_ready"), c_gh)
                        TT(X["reff"][:, t0:t0 + n], bank[4 * li][:, 0:n], AR[:, 1, t0:t0 + n], ALU.add)
                        rv, rw = bank[4 * li + 1], bank[4 * li + 3]
                        if n == 128:
                            for c in range(2):
                                e, src = t0 + RCH * (c + 1), (rv, rw)[c]
                                TT(Gt[:, 2 * t + c, :], src[:, 0:64], id64[:, :], ALU.add)
                                last = TS_(PH[:, 2 * t + c, :], src[:, 64:128], X["Ep"][:, e - 1:e], None, ALU.mult)
                        else:
                            TT(GtS[:, :, :], rv[:, :].rearrange("p (c d) -> p c d", c=NB),
                               id64[:, :].unsqueeze(1).to_broadcast([128, NB, 64]), ALU.add)
                            last = TT(PHS[:, :, :], rw[:, :].rearrange("p (c d) -> p c d", c=NB),
                                      X["Ep"][:, SEQ + NS - 1:NT:NS].unsqueeze(2).to_broadcast([128, NB, 64]), ALU.mult)
                        last.then_inc(S("gh_copied"), 1)
                        own(S("gh_copied"))
                dve.wait_ge(S("gh_copied"), c_gh)
                if p:
                    dve.wait_ge(s_out, 16 * (11 + 2 * p))
                dve.tensor_copy(Sst[:, 0, :], PH[:, 0, :]).then_inc(S("state_ready"), 1)
                own(S("state_ready"))
                for c in range(1, 8):
                    c_st += 1
                    e = RCH * (c + 1)
                    dve.wait_ge(S("state_step"), c_st)
                    STT(out=Sst[:, c, :], in0=bank[c % 2][:, 0:64], scalar=X["Ep"][:, e - 1:e], in1=PH[:, c, :],
                        op0=ALU.mult, op1=ALU.add).then_inc(S("state_ready"), 1)
                    own(S("state_ready"))
                dve.wait_ge(S("sstep_done"), p + 1)
                link(TT(SsS[:, :, :], bank[2][:, :].rearrange("p (c d) -> p c d", c=NB),
                        X["Ep"][:, SEQ + NS - 1:NT:NS].unsqueeze(2).to_broadcast([128, NB, 64]), ALU.mult))
                TT(SsS[:, :, :], SsS[:, :, :], PHS[:, :, :], ALU.add).then_inc(S("rstate_ready"), 1)
                own(S("rstate_ready"))
                dve.wait_ge(S("y_inter"), p + 1)
                dve.wait_ge(S("y0_ready"), c_gh)
                link(TT(X["y"][:, RCH:SEQ], bank[3][:, RCH:SEQ], X["y"][:, RCH:SEQ], ALU.add))
                TT(X["y"][:, SEQ:NT], bank[4][:, 0:SAMP], X["y"][:, SEQ:NT], ALU.add).then_inc(S("y_full"), 1)
                own(S("y_full"))
                dve.wait_ge(S("gmean_done"), p + 1)
                for dst, src in zip(main_samp(X["y"]), (bank[5][:, :], bank[6][:, 0:SAMP])):
                    link(STT(out=dst, in0=src, scalar=-1.0 / 64, in1=dst, op0=ALU.mult, op1=ALU.add))
                TT(X["kk"][:, :], X["y"][:, :], X["y"][:, :], ALU.mult).then_inc(S("gsq_ready"), 1)
                own(S("gsq_ready"))
                dve.wait_ge(S("gstd_ready"), p + 1)
                link(dve.reciprocal(X["d"][:, :], X["d"][:, :]))
                link(STT(out=X["y"][:, :], in0=X["y"][:, :], scalar=pcol("gn_g", p), in1=X["d"][:, :], op0=ALU.mult, op1=ALU.mult))
                link(STT(out=X["y"][:, :], in0=X["y"][:, :], scalar=pcol("gn_b", p), in1=X["bv"][:, :], op0=ALU.add, op1=ALU.add))
                TT(mixT[:, 4 + p, :], X["y"][:, :], X["gv"][:, :], ALU.mult).then_inc(S("mix_ready"), 1)
                own(S("mix_ready"))
                dve.wait_ge(S("mix_ready"), 5 + p)
            dve.wait_ge(s_x1, 16 * 7)
            for half in range(2):
                for t, (t0, n) in enumerate(TILES):
                    jj = 5 * half + t
                    cs = slice(512 * half, 512 * half + 512)
                    dve.wait_ge(S("outproj_done"), jj + 1)
                    TT(x1[0:n, t, cs], bank[jj % 4][0:n, :], x1[0:n, t, cs], ALU.add).then_inc(S("x1_ready"), 1)
                    own(S("x1_ready"))
            for t, (t0, n) in enumerate(TILES):
                dve.wait_ge(S("frms_ready"), t + 1)
                link(dve.reciprocal(st[0:n, t, 1:2], st[0:n, t, 1:2]))
                STT(out=xf[0:n, t, :], in0=x1[0:n, t, :], scalar=st[0:n, t, 1:2], in1=gb[0:n, 0, :], op0=ALU.mult, op1=ALU.mult
                    ).then_inc(S("xf_ready"), 1)
                own(S("xf_ready"))
            dve.wait_ge(S("iota_ready"), 1)

            def top16(val, ind, src, tmp):
                link(dve.max(val[:, 0:8], src))
                link(dve.max_index(ind[:, 0:8], val[:, 0:8], src))
                link(dve.match_replace(tmp, val[:, 0:8], src, -3.0e38))
                link(dve.max(val[:, 8:16], tmp))
                link(dve.max_index(ind[:, 8:16], val[:, 8:16], tmp))

            for t, (t0, n) in enumerate(TILES):
                dve.wait_ge(S("scores_ready"), t + 1)
                for j in range(16):
                    top16(sv[0:n, j, :], si[0:n, j, :], sc[0:n, 128 * j:128 * j + 128], sc2[0:n, 128 * j:128 * j + 128])
                link(dve.tensor_copy(sif[0:n, :, :], si[0:n, :, :]))
                for h in range(HEADS):
                    link(TT(sc[0:n, 256 * h:256 * h + 256].rearrange("p (a b) -> p a b", a=16),
                            sv[0:n, 2 * h, :].unsqueeze(2).to_broadcast([n, 16, 16]),
                            sv[0:n, 2 * h + 1, :].unsqueeze(1).to_broadcast([n, 16, 16]), ALU.add))
                for h in range(HEADS):
                    top16(cv[0:n, h, :], ci[0:n, h, :], sc[0:n, 256 * h:256 * h + 256], sc2[0:n, 256 * h:256 * h + 256])
                cif = ci[0:n, :, :].rearrange("p h k -> p (h k)")
                link(TS_(cab[0:n, 0, :], cif, 4, None, ALU.logical_shift_right))
                link(TS_(cab[0:n, 1, :], cif, 15, None, ALU.bitwise_and))
                link(dve.tensor_copy(cabf[0:n, :, :], cab[0:n, :, :]))
                for side in range(2):
                    hot = sc[0:n, :].rearrange("p (k j) -> p k j", j=16)
                    link(TT(hot, cabf[0:n, side, :].unsqueeze(2).to_broadcast([n, 128, 16]),
                            io16[0:n, :].unsqueeze(1).to_broadcast([n, 128, 16]), ALU.is_equal))
                    hot4 = sc[0:n, :].rearrange("p (h k j) -> p h k j", h=HEADS, k=16)
                    link(TT(hot4, hot4, sif[0:n, side:16:2, :].unsqueeze(2).to_broadcast([n, HEADS, 16, 16]), ALU.mult))
                    link(dve.tensor_reduce(isel[0:n, side, :], hot, AX.X, ALU.add))
                link(STT(out=isel[0:n, 0, :], in0=isel[0:n, 0, :], scalar=128.0, in1=isel[0:n, 1, :], op0=ALU.mult, op1=ALU.add))
                link(dve.tensor_copy(idx[0:n, t, :], isel[0:n, 0, :]))
                gt = gate[0:n, t, :].rearrange("p (h k) -> p h k", h=HEADS)
                TT(gt, cv[0:n, :, :], cv[0:n, :, 0:1].to_broadcast([n, HEADS, 16]), ALU.subtract).then_inc(S("shifted"), 1)
                own(S("shifted"))
                dve.wait_ge(S("gexp_ready"), t + 1)
                link(dve.tensor_reduce(mx8[0:n, 0, :], gt, AX.X, ALU.add))
                link(dve.reciprocal(mx8[0:n, 1, :], mx8[0:n, 0, :]))
                TT(gt, gt, mx8[0:n, 1, :].unsqueeze(2).to_broadcast([n, HEADS, 16]), ALU.mult).then_inc(S("routed"), 1)
                own(S("routed"))
            dve.wait_ge(S("routed"), 5)
            dve.memset(zer[:, :], 0.0).then_inc(S("zeros_ready"), 1)
            own(S("zeros_ready"))
            dve.sem_inc(S("u_used"), LEAD)
            dve.sem_inc(S("v_used"), LEAD)
            dve.sem_inc(S("gather_start"), 1)
            for t, (t0, n) in enumerate(TILES):
                with dve.Fori(0, HEADS // 2) as i:
                    for hh in range(2):
                        g0 = 128 * t + 16 * hh
                        for j in range(16):
                            dve.wait_ge(S(f"u_loaded{j % RING}"), loaded_count(i, g0, j))
                            STT(out=ub[0:n, j % RING, :], in0=ub[0:n, j % RING, :], scalar=1.0, in1=xf[0:n, t, :], op0=ALU.mult,
                                op1=ALU.mult, accum_out=dots[0:n, hh, j:j + 1]).then_inc(S("u_used"), 1)
                        dve.wait_ge(S("gelu_ready"), i * 2 + (8 * t + hh + 1))
                        TT(wts[0:n, hh, :], gel[0:n, hh, :], gate[0:n, t, bass.ds(i * 32 + 16 * hh, 16)], ALU.mult
                           ).then_inc(S("weight_ready"), 1)
                dve.wait_ge(S("acc_done"), t + 1)
                for half in range(2):
                    cs = slice(512 * half, 512 * half + 512)
                    last = TT(x1[0:n, t, cs], bank[2 * (t % 2) + half][0:n, :], x1[0:n, t, cs], ALU.add)
                last.then_inc(S("x2_ready"), 1)
                own(S("x2_ready"))
                dve.wait_ge(S("yrms_ready"), t + 1)
                link(dve.reciprocal(st[0:n, t, 3:4], st[0:n, t, 3:4]))
                STT(out=x1[0:n, t, :], in0=x1[0:n, t, :], scalar=st[0:n, t, 3:4], in1=gb[0:n, 1, :], op0=ALU.mult, op1=ALU.mult
                    ).then_inc(S("y_ready"), 1)
                own(S("y_ready"))


_OUTS = [("y", (NT, D)), ("cn_p", (128, MLH, 129)), ("m", (4, 1 + NB)), ("conv", (128, 8, 1 + NB, 3)),
         ("s_p", (128, 4, 64)), ("shift", (128, RT_TILES, 1 + NB)), ("cn_s", (128, MLH, NB, 129)),
         ("s_s", (128, 4, NB, 64))]


def kernel(**inputs):
    import numpy as np
    import concourse.bacc as bacc
    from concourse.bass_utils import run_bass_kernel_spmd

    I = {k: np.asarray(v) for k, v in inputs.items()}
    tiles = lambda a: np.asarray(a).reshape(-1, 128).T
    x = np.concatenate([I["x_prompt"].reshape(SEQ, D), I["x_sample"].reshape(SAMP, D)])
    par = np.concatenate(
        [tiles(I["norm_mix_g"][0]), tiles(I["ml_conv_w"][0]), tiles(I["ml_conv_b"][0]), tiles(I["ml_norm_g"][0]),
         tiles(I["rw_mu"][0]), tiles(I["rw_w0"][0]), tiles(I["rw_a0"][0]), tiles(I["rw_k_k"][0]), tiles(I["rw_k_a"][0]),
         tiles(I["rw_r_k"][0]), tiles(I["rw_gn_g"][0]), tiles(I["rw_gn_b"][0])], axis=1)
    small = np.concatenate([I["ml_b_i"].T, I["ml_b_f"].T, I["state_mlstm_m"][0].T], axis=1)
    conv0 = I["state_mlstm_conv"][0].reshape(NB, 3, 8, 128).transpose(3, 2, 0, 1)
    shift0 = I["state_rwkv_shift"][0].reshape(NB, RT_TILES, 128).transpose(2, 1, 0)
    cn0 = np.concatenate([I["state_mlstm_C"][0].transpose(2, 0, 1, 3), I["state_mlstm_n"][0].transpose(2, 0, 1)[..., None]], axis=3)
    s0 = I["state_rwkv_S"][0].reshape(NB, 4, 2, 64, 64).transpose(2, 4, 0, 1, 3).reshape(128, NB, 4, 64)
    sub = I["peer_sub_keys"][0].reshape(16, 128, 128).transpose(2, 0, 1)
    ins = [("xT", x.T), ("x", x), ("par", par), ("small", small), ("conv0", conv0), ("shift0", shift0), ("cn0", cn0),
           ("s0", s0), ("w_in", I["w_in"][0]), ("w2", I["rw_w2"][0]), ("a2", I["rw_a2"][0]), ("g2", I["rw_g2"][0]),
           ("w_out", I["w_out"][0]), ("gffn", I["norm_ffn_g"][0]), ("gfin", I["norm_final_g"]),
           ("w_q", I["peer_w_q"][0]), ("sub", sub), ("pu", I["peer_u"][0]), ("pv", I["peer_v"][0])]
    nc = bacc.Bacc("TRN2", target_bir_lowering=False, num_devices=1)
    arrays, args = {}, []
    for name, a in ins:
        a = np.ascontiguousarray(a)
        arrays["in_" + name] = a
        args.append(nc.dram_tensor("in_" + name, a.shape, mybir.dt.from_np(a.dtype), kind="ExternalInput").ap())
    for name, shape in _OUTS:
        args.append(nc.dram_tensor("out_" + name, shape, mybir.dt.float32, kind="ExternalOutput").ap())
    hybrid_step(nc, *args)
    r = run_bass_kernel_spmd(nc, [arrays], core_ids=[0])
    o = {name: r.results[0]["out_" + name] for name, _ in _OUTS}
    cnp = o["cn_p"].transpose(1, 0, 2)
    cns = o["cn_s"].transpose(2, 1, 0, 3)
    conv = o["conv"].transpose(2, 3, 1, 0).reshape(1 + NB, 3, 1024)
    shift = o["shift"].transpose(2, 1, 0).reshape(1 + NB, RT_TILES * 128)
    unpair = lambda s: s.reshape(2, 64, 4, -1, 64).transpose(3, 2, 0, 4, 1).reshape(-1, 8, 64, 64)
    m = o["m"].T
    c = np.ascontiguousarray
    return (c(o["y"][0:SEQ].reshape(1, SEQ, D)), c(o["y"][SEQ:].reshape(NB, NS, D)),
            c(cnp[None, None, :, :, 0:128]), c(cnp[None, None, :, :, 128]), c(m[None, 0:1]), c(conv[None, 0:1]),
            c(unpair(o["s_p"])[None]), c(shift[None, 0:1]),
            c(cns[None, :, :, :, 0:128]), c(cns[None, :, :, :, 128]), c(m[None, 1:]), c(conv[None, 1:]),
            c(unpair(o["s_s"])[None]), c(shift[None, 1:]))
```

```python
import concourse.bass as bass
from concourse import mybir
from contextlib import ExitStack
import math

D = 1024
SEQ = 512
NB, NS = 8, 8
SAMP = NB * NS
NT = SEQ + SAMP
KD = D // 128
MLH = 4
NE = 128 * 128
PT = SEQ // 128
TILES = [(t * 128, 128) for t in range(PT)] + [(SEQ, SAMP)]
MCH = 128
RCH = 64
CW = 4
RT_TILES = 14
EXQ = 3 + SEQ + NB * (NS + 3)
EXR = 1 + SEQ + NB * (NS + 1)
HEADS, TOPK = 8, 16
GE = 4
EG = NE // 128 // GE
GU = 2
UG = NE // 128 // GU
PLAIN = [6, 6, 6, 6, 4]
GATED = [8, 8, 8, 8, 4]
PLAIN0 = [sum(PLAIN[:t]) + sum(GATED[:t]) for t in range(5)]
GATED0 = [PLAIN0[t] + PLAIN[t] for t in range(5)]
assert PLAIN0[4] + PLAIN[4] + GATED[4] == UG
QG = 4
GC = 32
NCH = NT // GC
HN = NT // 2
NEG = -1.0e30
ML_END = 2056
PCOL = {}
_at = 0
for _n, _w in [("g_mix", 8), ("conv_w", 32), ("conv_b", 8), ("ml_g", 4), ("mu", 14), ("w0", 4), ("a0", 4),
               ("k_k", 4), ("k_a", 4), ("r_k", 4), ("gn_g", 4), ("gn_b", 4)]:
    PCOL[_n] = _at
    _at += _w
NPAR = _at


def hybrid_step(nc, xT_d, x_d, par_d, small_d, conv0_d, shift0_d, cn0_d, s0_d, w_in, w2_d, a2_d, g2_d,
                w_out, gffn_d, gfin_d, w_q, sub_d, pu, pv,
                y_o, cn_p_o, m_o, conv_o, s_p_o, shift_o, cn_s_o, s_s_o):
    f32 = mybir.dt.float32
    f32r = mybir.dt.float32r
    u32 = mybir.dt.uint32
    ALU = mybir.AluOpType
    ACT = mybir.ActivationFunctionType
    AX = mybir.AxisListType

    ctx = ExitStack()
    with ctx:
        def sb(name, shape, dt=f32, scope=ctx):
            return scope.enter_context(nc.sbuf_tensor(name, shape, dt))

        def sem(name):
            return ctx.enter_context(nc.semaphore(name))

        bank = [ctx.enter_context(nc.psum_tensor(f"bank{i}", [128, 512], f32)) for i in range(8)]

        ident = sb("ident", [128, 128])
        ones = sb("ones", [128, 128])
        eps_t = sb("eps_t", [128, 4])
        mix_sc = ExitStack()
        mixT = sb("mixT", [128, KD, NT], scope=mix_sc)
        mix_sc.close()
        xlo = sb("xlo", [128, KD, NT], f32r)
        mixers = ExitStack()
        blk = sb("blk", [128, 128], scope=mixers)
        id64 = sb("id64", [128, 64], scope=mixers)
        negm = sb("negm", [128, 128], scope=mixers)
        negs = sb("negs", [64, 64], scope=mixers)
        seqm = sb("seqm", [64, NB], scope=mixers)
        mask4 = sb("mask4", [128, 4, 128], scope=mixers)
        mask4s = sb("mask4s", [64, 4, 64], scope=mixers)
        mask3 = sb("mask3", [128, 3, 128], scope=mixers)
        masks = sb("masks", [64, 64], scope=mixers)
        mtmp = sb("mtmp", [128, 3, 128], scope=mixers)
        selr = sb("selr", [4, MLH, 128], scope=mixers)
        rst_m = sb("rst_m", [4, NT], scope=mixers)
        rst_r = sb("rst_r", [128, NT], scope=mixers)
        par = sb("par", [128, NPAR], scope=mixers)
        small = sb("small", [4, 2 + NB], scope=mixers)
        cn0 = sb("cn0", [128, NB, MLH, 129], scope=mixers)
        s0 = sb("s0", [128, NB, 4, 64], scope=mixers)
        w2 = sb("w2", [64, 512], scope=mixers)
        a2 = sb("a2", [128, 512], scope=mixers)
        g2 = sb("g2", [128, 512], scope=mixers)
        ext_r = sb("ext_r", [128, RT_TILES, EXR], scope=mixers)
        shift_t = sb("shift_t", [128, RT_TILES, 1 + NB], scope=mixers)
        mlstm = ExitStack()
        ext_q = sb("ext_q", [128, 8, EXQ], scope=mlstm)
        vaug = sb("vaug", [128, 5, MLH, 129], scope=mlstm)
        osig = sb("osig", [128, MLH, NT], scope=mlstm)
        gi = sb("gi", [4, NT], scope=mlstm)
        gf = sb("gf", [4, NT], scope=mlstm)
        conv_t = sb("conv_t", [128, 8, 1 + NB, 3], scope=mlstm)
        proj = ExitStack()
        xnT = sb("xnT", [128, KD, NT], scope=proj)
        wbuf = [sb(f"wbuf{i}", [128, KD, 512], scope=proj) for i in range(2)]
        conv0 = sb("conv0", [128, 8, NB, 3], scope=proj)
        shift0 = sb("shift0", [128, RT_TILES, NB], scope=proj)
        rb = sb("rb", [128, NT], scope=proj)
        sq = sb("sq", [128, 2, NT], scope=proj)
        proj.close()
        mw = ExitStack()
        rows = {n: sb("row_" + n, [4, NT], scope=mw) for n in ["l", "b", "m", "E1", "E2", "Ks", "W", "flo"]}
        mo = sb("mo", [4, 1 + NB], scope=mw)
        mcol = sb("mcol", [128, 5, 2, 4], scope=mw)
        wcolX = sb("wcolX", [64, MLH, NB], scope=mw)
        pre = sb("pre", [128, 2, NT], scope=mw)
        sg = sb("sg", [128, 2, NT], scope=mw)
        qh = sb("qh", [128, NT], scope=mw)
        kh = sb("kh", [128, NT], scope=mw)
        qs = sb("qs", [128, NT], scope=mw)
        qn = sb("qn", [128, NT], scope=mw)
        bc = sb("bc", [128, 3, NT], scope=mw)
        ktok = sb("ktok", [128, 5, 128], scope=mw)
        dmat = sb("dmat", [128, 5, 128], scope=mw)
        pmat = sb("pmat", [128, 5, 128], scope=mw)
        wv = sb("wv", [128, PT, 129], scope=mw)
        wvX = sb("wvX", [64, NB, 129], scope=mw)
        cn = sb("cn", [128, PT, 129], scope=mw)
        cnS = sb("cnS", [128, NB, 129], scope=mw)
        hb, hq, hr = pre[:, 0, :], pre[:, 1, :], sg[:, 0, :]
        mw.close()
        mlstm.close()
        rwk = ExitStack()
        xwa = sb("xwa", [128, NT], scope=rwk)
        xg = sb("xg", [128, NT], scope=rwk)
        X = {n: sb("rw_" + n, [128, NT], scope=rwk) for n in
             ["d", "r", "k", "v", "sw", "av", "gv", "cum", "cm", "Ep", "En", "kk", "t", "kf",
              "be", "ka", "bv", "reff", "y"]}
        AR = sb("rw_AR", [128, 2, NT], scope=rwk)
        tok4 = sb("tok4", [128, 2, 4, 128], scope=rwk)
        G4 = [sb(f"G4_{u}", [128, 4, 128], scope=rwk) for u in range(4)]
        M3 = [sb(f"M3_{u}", [128, 3, 128], scope=rwk) for u in range(4)]
        XM = [[sb(f"XM{u}_{i}", [128, 3, 128], scope=rwk) for i in range(2)] for u in range(4)]
        TB = [sb(f"TB{u}", [128, 2, 128], scope=rwk) for u in range(4)]
        NV = [sb(f"NV{u}", [128, 64], scope=rwk) for u in range(4)]
        TS = [sb(f"TS{u}", [128, 128], scope=rwk) for u in range(4)]
        bX = sb("bX", [64, NB, 128], scope=rwk)
        kX = sb("kX", [64, NB, 128], scope=rwk)
        Gt = sb("Gt", [128, 8, 64], scope=rwk)
        PH = sb("PH", [128, 8, 64], scope=rwk)
        GtS = sb("GtS", [128, 8, 64], scope=rwk)
        PHS = sb("PHS", [128, 8, 64], scope=rwk)
        Sst = sb("Sst", [128, 8, 64], scope=rwk)
        SsS = sb("SsS", [128, 8, 64], scope=rwk)
        rwk.close()
        mixers.close()
        pe_sc = ExitStack()
        gain = sb("gain", [128, D], scope=pe_sc)
        gate = sb("gate", [128, 5, HEADS * TOPK], scope=pe_sc)
        st = sb("st", [128, 5, 4], scope=pe_sc)
        panels = ExitStack()
        wring = sb("wring", [128, 2, KD, 512], scope=panels)
        panels.close()
        u_raw = sb("u_raw", [128, 2, KD, GU * 128], scope=pe_sc)
        u_lo = sb("u_lo", [128, 2, KD, GU * 128], f32r, scope=pe_sc)
        w_flat = wring[:, :, :, :].rearrange("p a k n -> p (a k n)")
        v_raw = w_flat.rearrange("p (s n) -> p s n", s=2)
        x1_late = w_flat[:, 0:5 * D].rearrange("p (t d) -> p t d", t=5)
        sq_late = w_flat[:, 5 * D:6 * D]
        acc = mixT
        xfT = mixT
        first = ExitStack()
        x1_sc = ExitStack()
        x1 = sb("x1", [128, 5, D], scope=x1_sc)
        x1_sc.close()
        u_hi = sb("u_hi", [128, 2, KD, GU * 128], f32r, scope=first)
        pad = sb("pad", [128, D], scope=first)
        xhi = sb("xhi", [128, KD, NT], f32r, scope=first)
        sub_sc = ExitStack()
        subT = sb("subT", [128, 16, 128], scope=sub_sc)
        sub_sc.close()
        actb = sb("actb", [128, 2, GU, NT], scope=first)
        early = ExitStack()
        qT = sb("qT", [128, 16, NT], scope=early)
        early.close()
        norms = ExitStack()
        xf = sb("xf", [128, 2, D], scope=norms)
        sqs = sb("sqs", [128, D], scope=norms)
        norms.close()
        gst = sb("gst", [128, 2, 128, GC], scope=first)
        hot_b = sb("hot_b", [128, 8, 128], f32r, scope=first)
        hot_a = sb("hot_a", [128, 2, 8, 128], f32r, scope=first)
        hkT = sb("hkT", [128, 3, 128], scope=first)
        hk_hi = sb("hk_hi", [128, 128], f32r, scope=first)
        io128 = sb("io128", [128, 128], scope=first)
        sca = sb("sca", [128, 5, 2048], scope=first)
        sc2 = sb("sc2", [128, 256], scope=first)
        sv = sb("sv", [128, 16, 16], scope=first)
        si = sb("si", [128, 16, 16], u32, scope=first)
        sif = sb("sif", [128, 16, 16], scope=first)
        cv = sb("cv", [128, HEADS, 16], scope=first)
        ci = sb("ci", [128, HEADS, 16], u32, scope=first)
        cab = sb("cab", [128, 2, HEADS * 16], u32, scope=first)
        cabf = sb("cabf", [128, 2, HEADS * 16], scope=first)
        isel = sb("isel", [128, 2, HEADS * 16], scope=first)
        mx8 = sb("mx8", [128, 2, HEADS], scope=first)
        first.close()
        second = ExitStack()
        v_hi = sb("v_hi", [128, 2, GE * D], f32r, scope=second)
        v_lo = sb("v_lo", [128, 2, GE * D], f32r, scope=second)
        wts = sb("wts", [128, 2, GE, NT], scope=second)
        w_hi = sb("w_hi", [128, 2, GE, NT], f32r, scope=second)
        w_lo = sb("w_lo", [128, 2, GE, NT], f32r, scope=second)
        gring = sb("gring", [128, 2, NCH, GE, GC], scope=second)
        second.close()
        pe_sc.close()
        io16 = io128[:, 0:16]
        x1_d = nc.dram_tensor("residual_scratch", [NT, D], f32, kind="Internal").ap()
        act_d = nc.dram_tensor("act_scratch", [EG, 128, GE * NT], f32, kind="Internal").ap()
        gate_d = nc.dram_tensor("gate_scratch", [NCH, 128, 128, GC], f32, kind="Internal").ap()

        def pcol(name, t):
            return par[:, PCOL[name] + t:PCOL[name] + t + 1]

        s_par, s_x, s_w, s_init = sem("par_loaded"), sem("xT_loaded"), [sem("w_loaded0"), sem("w_loaded1")], sem("state_loaded")
        s_out = sem("stores_done")
        s_ring = [sem("ring_loaded0"), sem("ring_loaded1")]
        s_x1 = sem("x_loaded")
        s_sub = sem("subkeys_loaded")
        s_v = [sem("v_loaded0"), sem("v_loaded1")]
        s_act = [sem("act_stored0"), sem("act_stored1")]
        s_gst = [sem("gates_stored0"), sem("gates_stored1")]
        s_x1s = sem("residual_stored")
        s_u = [sem("u_loaded0"), sem("u_loaded1")]
        s_grp = [sem("group_loaded0"), sem("group_loaded1")]
        c_dve, c_act, c_pool = sem("vector_step"), sem("scalar_step"), sem("gpsimd_step")
        s_const = sem("constants_ready")
        s_sq, s_sqf, s_sd, s_xn = sem("squares_ready"), sem("squares_summed"), sem("rms_ready"), sem("xn_ready")
        s_pj, s_pe = sem("proj_done"), sem("proj_copied")
        held = {}

        def S(name):
            if name not in held:
                held[name] = sem(name)
            return held[name]

        block = ctx.enter_context(nc.Block())

        PANELS = [(0, 512), (512, 512), (1024, 512), (1536, 512), (2048, 8),
                  (ML_END, 512), (ML_END + 512, 512), (ML_END + 1024, 512), (ML_END + 1536, 256)]
        JOBS = []
        for p in (0, 1):
            JOBS += [("q", p, 128 * j, 128, 4 * p + j) for j in range(4)]
        JOBS += [("v", 2, 0, 512, t) for t in range(5)]
        JOBS += [("o", 3, 128 * j, 128, j) for j in range(4)]
        JOBS += [("i", 4, 0, 4, 0), ("f", 4, 4, 4, 0)]
        for p in range(5, 9):
            JOBS += [("r", p, 128 * j, 128, 4 * (p - 5) + j) for j in range(PANELS[p][1] // 128)]
        NJ = len(JOBS)

        def main_samp(ap):
            return [ap[:, 0:SEQ], ap[:, SEQ:NT]]

        GROUPS = [[0, 1], [2, 3], [4]]

        def units(g):
            return [(t, h) for t in GROUPS[g] for h in range(2)]

        ULIST = [(p, g, u) for p in range(4) for g in range(3) for u in range(len(units(g)))]

        @block.sync
        def _(sp):
            sp.dma_start(par[:, :], par_d).then_inc(s_par, 16)
            sp.dma_start(xnT[:, :, :], xT_d.rearrange("(k p) n -> p k n", p=128)).then_inc(s_x, 16)
            for p, (c0, w) in enumerate(PANELS):
                if p >= 2:
                    sp.wait_ge(s_pj, sum(j[1] <= p - 2 for j in JOBS))
                sp.dma_start(wbuf[p % 2][:, :, 0:w],
                             w_in.rearrange("(k p) n -> p k n", p=128)[:, :, c0:c0 + w]).then_inc(s_w[p % 2], 16)
                if p == 1:
                    for dst, src in [(small[:, :], small_d), (conv0[:, :, :, :], conv0_d), (shift0[:, :, :], shift0_d),
                                     (cn0[:, :, :, :], cn0_d), (s0[:, :, :, :], s0_d), (w2[:, :], w2_d),
                                     (a2[64:128, :], a2_d), (g2[:, :], g2_d)]:
                        sp.dma_start(dst, src).then_inc(s_init, 16)
            sp.wait_ge(S("m_ready"), 1)
            sp.dma_start(m_o, mo[:, :]).then_inc(s_out, 16)
            for h in range(MLH):
                sp.wait_ge(S("cn_ready"), h + 1)
                sp.dma_start(cn_p_o[:, h, :], cn[:, PT - 1, :]).then_inc(s_out, 16)
                sp.dma_start(cn_s_o[:, h, :, :], cnS[:, :, :]).then_inc(s_out, 16)
            sp.wait_ge(S("tails_ready"), 2)
            sp.dma_start(conv_o, conv_t[:, :, :, :]).then_inc(s_out, 16)
            sp.dma_start(shift_o, shift_t[:, :, :]).then_inc(s_out, 16)
            for p in range(4):
                sp.wait_ge(S("rstate_ready"), p + 1)
                sp.dma_start(s_p_o[:, p, :], Sst[:, 7, :]).then_inc(s_out, 16)
                sp.dma_start(s_s_o[:, p, :, :], SsS[:, :, :]).then_inc(s_out, 16)
            sp.wait_ge(S("mix_ready"), 8)
            sp.wait_ge(s_out, 16 * 19)
            for t, (t0, n) in enumerate(TILES):
                sp.dma_start(x1[0:n, t, :], x_d[t0:t0 + n, :]).then_inc(s_x1, 16)
            sp.dma_start(gain[:, :], gffn_d.partition_broadcast(128)).then_inc(s_x1, 16)
            sp.dma_start(subT[:, :, :], sub_d).then_inc(s_sub, 16)
            for i in range(6):
                if i >= 2:
                    sp.wait_ge(S("outproj_done" if i < 4 else "qproj_done"), 5 * (i - 1) if i < 4 else 4 * (i - 3))
                src, c = (w_out, i) if i < 2 else (w_q, i - 2)
                sp.dma_start(wring[:, i % 2, :, :], src.rearrange("(k p) n -> p k n", p=128)[:, :, 512 * c:512 * c + 512]
                             ).then_inc(s_ring[i % 2], 16)
            sp.wait_ge(S("x1_ready"), 10)
            for t, (t0, n) in enumerate(TILES):
                sp.dma_start(x1_d[t0:t0 + n, :], x1[0:n, t, :]).then_inc(s_x1s, 16)
            sp.wait_ge(S("qproj_done"), 12)
            for g in range(2):
                sp.dma_start(u_raw[:, g, :, :], pu[g]).then_inc(s_u[g], 16)
            with sp.Fori(0, UG // 2 - 1) as i:
                for q in range(2):
                    sp.wait_ge(S("u_lo_ready"), i * 2 + (q + 1))
                    sp.sem_inc(S("u_slot_seen"), 1)
                    sp.dma_start(u_raw[:, q, :, :], pu[bass.ds(i * 2 + (2 + q), 1)].squeeze(0)).then_inc(s_u[q], 16)
            sp.wait_ge(S("dots_done"), 2 * GU + GU * UG)
            sp.wait_ge(S("gmat_done"), NT // 4)
            sp.wait_ge(S("xf_ready"), 5)
            sp.dma_start(gain[:, :], gfin_d.partition_broadcast(128)).then_inc(s_x1, 16)
            for q in range(2):
                sp.wait_ge(s_act[q], 16 * (UG // 2 + 1))
                sp.wait_ge(s_gst[q], 16 * (NCH // 2 + 1))

            def load_group(q, v_src, a_src, g_src):
                sp.dma_start(wts[:, q, :, :].rearrange("p e n -> p (e n)"), a_src).then_inc(s_grp[q], 16)
                sp.dma_start(gring[:, q, :, :, :].rearrange("p c e t -> p c (e t)"), g_src).then_inc(s_grp[q], 16)
                sp.dma_start(v_raw[:, q, :], v_src).then_inc(s_v[q], 16)

            gate_v = gate_d.rearrange("c p (g e) t -> g p c (e t)", e=GE)
            for q in range(2):
                load_group(q, pv[q], act_d[q], gate_v[q])
            with sp.Fori(0, EG // 2 - 1) as i:
                for q in range(2):
                    sp.wait_ge(S("w_lo_ready"), i * 2 + (q + 1))
                    sp.wait_ge(S("v_lo_ready"), i * 2 + (q + 1))
                    sp.sem_inc(S("v_slot_seen"), 1)
                    g = bass.ds(i * 2 + (2 + q), 1)
                    load_group(q, pv[g].squeeze(0), act_d[g].squeeze(0), gate_v[g].squeeze(0))
            sp.wait_ge(S("v_lo_ready"), EG)
            sp.wait_ge(s_x1s, 16 * 5)
            for t, (t0, n) in enumerate(TILES):
                sp.dma_start(x1_late[0:n, t, :], x1_d[t0:t0 + n, :]).then_inc(s_x1, 16)
            for t, (t0, n) in enumerate(TILES):
                sp.wait_ge(S("y_ready"), t + 1)
                sp.dma_start(y_o[t0:t0 + n, :], x1_late[0:n, t, :]).then_inc(s_out, 16)
            sp.wait_ge(s_out, 16 * (19 + 5))

        @block.gpsimd
        def _(pool):
            k = [0]

            def link(ins):
                k[0] += 1
                ins.then_inc(c_pool, 1)
                pool.wait_ge(c_pool, k[0])

            def select(out, pattern, base, mult, fill, op=ALU.is_ge):
                link(pool.affine_select(out=out, in_=out, compare_op=op, fill=fill, base=base,
                                        pattern=pattern, channel_multiplier=mult))

            link(pool.memset(ident[:, :], 0.0))
            select(ident[:, :], [[-1, 128]], 0, 1, 1.0, ALU.not_equal)
            link(pool.memset(ones[:, :], 1.0))
            link(pool.memset(eps_t[:, 0:1], 1e-6))
            link(pool.memset(eps_t[:, 1:2], 64 * 1e-5))
            link(pool.memset(eps_t[:, 2:3], 1.0))
            pool.memset(eps_t[:, 3:4], 0.0).then_inc(s_const, 1)
            link(pool.memset(ext_q[:, :, 0:3], 0.0))
            link(pool.memset(ext_r[:, :, 0:1], 0.0))
            link(pool.memset(vaug[:, :, :, 128:129], 1.0))
            def block_ones(out, p, n, w):
                link(pool.memset(out, 1.0))
                v = out.rearrange("p (c w) -> p c w", w=w)
                select(v, [[-w, n // w], [0, w]], 0, 1, 0.0)
                select(v, [[w, n // w], [0, w]], w - 1, -1, 0.0)
            block_ones(blk[:, :], 128, 128, 64)
            link(pool.memset(id64[:, :], 0.0))
            select(id64[:, :], [[-1, 64]], 0, 1, 1.0, ALU.not_equal)
            select(id64[:, :], [[-1, 64]], -64, 1, 1.0, ALU.not_equal)
            link(pool.memset(negm[:, :], 0.0))
            select(negm[:, :], [[1, 128]], 0, -1, NEG)
            link(pool.memset(negs[:, :], 0.0))
            select(negs[:, :], [[1, 64]], 0, -1, NEG)
            select(negs[:, :].rearrange("p (c w) -> p c w", w=8), [[-8, 8], [0, 8]], 0, 1, NEG)
            select(negs[:, :].rearrange("p (c w) -> p c w", w=8), [[8, 8], [0, 8]], 7, -1, NEG)
            link(pool.memset(seqm[:, :], 1.0))
            select(seqm[:, :], [[-8, 8]], 0, 1, 0.0)
            select(seqm[:, :], [[8, 8]], 7, -1, 0.0)
            for i, w in enumerate((16, 32, 64)):
                block_ones(mtmp[:, i, :], 128, 128, w)
            for i in range(3):
                link(pool.tensor_copy(mask3[:, i, :], mtmp[:, i, :]))
            for i in (1, 2):
                link(pool.tensor_tensor(mask3[:, i, :], mtmp[:, i, :], mtmp[:, i - 1, :], ALU.subtract))
            select(mask3[:, :, :], [[0, 3], [-1, 128]], -1, 1, 0.0)
            link(pool.tensor_copy(mask4[:, 0, :], mtmp[:, 0, :]))
            for i in (1, 2, 3):
                link(pool.tensor_copy(mask4[:, i, :], mtmp[:, 2, :]))
            for i, strict in enumerate((1, 0, 1, 0)):
                select(mask4[:, i, :], [[1, 128]], -strict, -1, 0.0)
            for i, strict in enumerate((1, 0, 1, 0)):
                block_ones(mask4s[:, i, :], 64, 64, 8)
                select(mask4s[:, i, :], [[1, 64]], -strict, -1, 0.0)
            block_ones(masks[:, :], 64, 64, 8)
            select(masks[:, :], [[-1, 64]], -1, 1, 0.0)
            link(pool.memset(selr[:, :, :], 0.0))
            select(selr[:, :, :], [[-1, MLH], [0, 128]], 0, 1, 1.0, ALU.not_equal)
            link(pool.memset(rst_m[:, :], 1.0))
            link(pool.memset(rst_m[:, 0:SEQ:MCH], 0.0))
            link(pool.memset(rst_m[:, SEQ:NT:NS], 0.0))
            link(pool.memset(rst_r[:, :], 1.0))
            link(pool.memset(rst_r[:, 0:SEQ:RCH], 0.0))
            pool.memset(rst_r[:, SEQ:NT:NS], 0.0).then_inc(s_const, 1)
            pool.wait_ge(S("mix_ready"), 8)
            pool.iota(io128[:, :], pattern=[[1, 128]], base=0, channel_multiplier=0,
                      allow_small_or_imprecise_dtypes=True).then_inc(S("iota_ready"), 1)
            pool.wait_ge(S("iota_ready"), 1)
            def split_u(g):
                pool.wait_ge(S("u_hi_ready"), g + 1)
                pool.tensor_tensor(u_lo[:, g % 2, :, :], u_raw[:, g % 2, :, :], u_hi[:, g % 2, :, :].bitcast(f32),
                                   ALU.subtract).then_inc(S("u_lo_ready"), 1)

            def hot_quad(quad):
                j = 4 * quad % 128
                if quad >= 2:
                    pool.wait_ge(S("gmat_done"), quad - 1)
                for m in range(3):
                    ins = pool.tensor_scalar(hot_b[:, 4 * (quad % 2) + m, :], io128[:, :], hkT[:, 1, j + m:j + m + 1], None,
                                             ALU.is_equal)
                ins.then_inc(S("hot_b_ready"), 1)

            split_u(0)
            for t in range(5):
                for g in range(PLAIN0[t], GATED0[t]):
                    split_u(g + 1)
                pool.wait_ge(S("hk_ready"), t + 1)
                for g in range(GATED0[t], GATED0[t] + GATED[t]):
                    quad = 32 * t + QG * (g - GATED0[t])
                    for i in range(QG):
                        hot_quad(quad + i)
                        if i == 1 and g + 1 < UG:
                            split_u(g + 1)
            with pool.Fori(0, EG // 2) as i:
                for q in range(2):
                    pool.wait_ge(S("v_hi_ready"), i * 2 + (q + 1))
                    pool.sem_inc(S("v_hi_seen"), 1)
                    pool.tensor_tensor(v_lo[:, q, :], v_raw[:, q, :], v_hi[:, q, :].bitcast(f32), ALU.subtract
                                       ).then_inc(S("v_lo_ready"), 1)

        @block.scalar
        def _(act):
            k = [0]

            def link(ins):
                k[0] += 1
                ins.then_inc(c_act, 1)
                act.wait_ge(c_act, k[0])

            raised = {}

            def own(signal):
                raised[signal.name] = raised.get(signal.name, 0) + 1
                act.wait_ge(signal, raised[signal.name])

            act.wait_ge(s_x, 16)
            act.wait_ge(s_const, 1)
            for kt in range(KD):
                if kt >= 2:
                    act.wait_ge(s_sqf, kt - 1)
                act.activation(sq[:, kt % 2, :], xnT[:, kt, :], ACT.Square).then_inc(s_sq, 1)
                own(s_sq)
            act.wait_ge(s_sqf, KD)
            for dst, b in zip(main_samp(rb), (0, 1)):
                act.activation(dst, bank[b][:, 0:dst.shape[1]], ACT.Sqrt, bias=eps_t[:, 0:1], scale=1.0 / D
                               ).then_inc(s_sd, 1)
                own(s_sd)
            act.wait_ge(s_init, 16 * 8)
            for ji, (kind, p, c0, w, d) in enumerate(JOBS):
                b = 2 * (ji % 2)
                act.wait_ge(s_pj, ji + 1)
                if kind == "v":
                    n = TILES[d][1]
                    act.activation(vaug[0:n, d, :, 0:128], bank[b][0:n, :].rearrange("p (h e) -> p h e", h=MLH),
                                   ACT.Copy).then_inc(s_pe, 1)
                    own(s_pe)
                    continue
                if kind in "if":
                    dst = gi if kind == "i" else gf
                    bias = small[:, 0:1] if kind == "i" else small[:, 1:2]
                    act.activation(dst[:, 0:SEQ], bank[b][0:4, :], ACT.Identity, bias=bias)
                    act.activation(dst[:, SEQ:NT], bank[b + 1][0:4, 0:SAMP], ACT.Identity, bias=bias).then_inc(s_pe, 1)
                    own(s_pe)
                    continue
                if kind == "o":
                    act.activation(osig[:, d, 0:SEQ], bank[b][:, :], ACT.Sigmoid)
                    act.activation(osig[:, d, SEQ:NT], bank[b + 1][:, 0:SAMP], ACT.Sigmoid).then_inc(s_pe, 1)
                    own(s_pe)
                    continue
                ext, lead = (ext_q, 3) if kind == "q" else (ext_r, 1)
                act.activation(ext[:, d, lead:lead + SEQ], bank[b][:, :], ACT.Copy)
                act.activation(ext[:, d, lead + SEQ:].rearrange("p (b s) -> p b s", b=NB)[:, :, lead:],
                               bank[b + 1][:, 0:SAMP].rearrange("p (b s) -> p b s", b=NB), ACT.Copy).then_inc(s_pe, 1)
                own(s_pe)
            act.wait_ge(S("gate_abs"), 1)
            link(act.activation(rows["l"][:, :], rows["l"][:, :], ACT.Exp, scale=-1.0))
            act.activation(rows["l"][:, :], rows["l"][:, :], ACT.Ln, bias=eps_t[0:4, 2:3]).then_inc(S("gate_log"), 1)
            own(S("gate_log"))
            act.wait_ge(S("rows_ready"), 1)
            act.activation(rows["E2"][:, :], rows["E2"][:, :], ACT.Exp)
            act.activation(rows["flo"][:, :], rows["m"][:, :], ACT.Exp, scale=-1.0)
            act.activation(rows["W"][:, :], rows["W"][:, :], ACT.Exp).then_inc(S("rows_exp"), 1)
            own(S("rows_exp"))
            for h in range(MLH):
                for i in range(3):
                    act.wait_ge(S("bcast_done"), 3 * h + i + 1)
                    b = 2 * (i % 2)
                    act.activation(bc[:, i, 0:SEQ], bank[b][:, :], ACT.Copy)
                    act.activation(bc[:, i, SEQ:NT], bank[b + 1][:, 0:SAMP], ACT.Copy).then_inc(S("bcast_copied"), 1)
                    own(S("bcast_copied"))
                for i in range(2):
                    act.wait_ge(S("conv_ready"), 2 * h + i + 1)
                    act.activation(sg[:, i, :], pre[:, i, :], ACT.Sigmoid).then_inc(S("conv_sig"), 1)
                    own(S("conv_sig"))
                act.wait_ge(S("ktok_done"), h + 1)
                act.activation(ktok[:, 0:PT, :], bank[4][:, :].rearrange("p (t d) -> p t d", t=PT), ACT.Copy)
                act.activation(ktok[0:SAMP, PT, :], bank[5][0:SAMP, 0:128], ACT.Copy).then_inc(S("ktok_ready"), 1)
                own(S("ktok_ready"))
                act.wait_ge(S("dlog_ready"), h + 1)
                act.activation(dmat[:, 0:PT, :], dmat[:, 0:PT, :], ACT.Exp)
                act.activation(dmat[0:SAMP, PT, 0:SAMP], dmat[0:SAMP, PT, 0:SAMP], ACT.Exp).then_inc(S("d_ready"), 1)
                own(S("d_ready"))
                act.wait_ge(S("var_done"), h + 1)
                act.activation(hr[:, 0:SEQ], bank[2][:, :], ACT.Sqrt, bias=eps_t[:, 0:1], scale=1.0 / 128)
                act.activation(hr[:, SEQ:NT], bank[3][:, 0:SAMP], ACT.Sqrt, bias=eps_t[:, 0:1], scale=1.0 / 128
                               ).then_inc(S("std_ready"), 1)
                own(S("std_ready"))
            act.wait_ge(S("lora_in"), 1)
            act.activation(xwa[0:64, :], xwa[0:64, :], ACT.Tanh)
            act.activation(xg[:, :], xg[:, :], ACT.Sigmoid).then_inc(S("lora_act"), 1)
            own(S("lora_act"))
            c_tok = c_stg = c_nv = c_mg = c_ts = c_y0 = 0
            for p in range(4):
                act.wait_ge(S("lora_done"), p + 1)
                for b, name, fn, bias in ((0, "sw", ACT.Sigmoid, "w0"), (2, "av", ACT.Sigmoid, "a0"), (4, "gv", ACT.Copy, None)):
                    for dst, src in zip(main_samp(X[name]), (bank[b][:, :], bank[b + 1][:, 0:SAMP])):
                        if bias:
                            ins = act.activation(dst, src, fn, bias=pcol(bias, p))
                        else:
                            ins = act.activation(dst, src, fn)
                ins.then_inc(S("lora_out"), 1)
                own(S("lora_out"))
                act.wait_ge(S("kk_clamped"), p + 1)
                act.activation(X["t"][:, :], X["t"][:, :], ACT.Sqrt).then_inc(S("kk_norm"), 1)
                own(S("kk_norm"))
                act.wait_ge(S("cum_ready"), p + 1)
                act.activation(X["Ep"][:, :], X["cum"][:, :], ACT.Exp)
                act.activation(X["En"][:, :], X["cum"][:, :], ACT.Exp, scale=-1.0)
                act.activation(X["cm"][:, :], X["cm"][:, :], ACT.Exp).then_inc(S("decay_ready"), 1)
                own(S("decay_ready"))
                for g, tiles in enumerate(GROUPS):
                    us = units(g)
                    n = TILES[tiles[0]][1]
                    for li, t in enumerate(tiles):
                        c_tok += 1
                        act.wait_ge(S("tok_done"), c_tok)
                        act.activation(tok4[0:n, li, :, :], bank[4 * li + 3][0:n, :].rearrange("p (a d) -> p a d", a=4),
                                       ACT.Copy).then_inc(S("tok_ready"), 1)
                        own(S("tok_ready"))
                    nst = 4 if n == 128 else 3
                    for u in range(len(us)):
                        c_nv += 1
                        act.wait_ge(S("nv_done"), c_nv)
                        act.activation(NV[u][0:n, :], bank[2 * u + 1][0:n, 0:64], ACT.Copy).then_inc(S("nv_ready"), 1)
                        own(S("nv_ready"))
                    for s in range(nst - 1):
                        for u in range(len(us)):
                            act.wait_ge(S("stage_done"), (c_stg := c_stg + 1))
                            act.activation(XM[u][s % 2][0:n, 0:2, 0:n],
                                           bank[2 * u][0:n, 0:2 * n].rearrange("p (a d) -> p a d", a=2),
                                           ACT.Copy).then_inc(S("powers_ready"), 1)
                            own(S("powers_ready"))
                    c_stg += len(us)
                    if n == 128:
                        for m in range(2):
                            for u in range(len(us)):
                                c_mg += 1
                                act.wait_ge(S("merge_a"), c_mg)
                                act.activation(TB[u][:, :, :], bank[2 * u][:, 0:256].rearrange("p (a d) -> p a d", a=2),
                                               ACT.Copy).then_inc(S("merge_b"), 1)
                                own(S("merge_b"))
                    for u in range(len(us)):
                        c_ts += 1
                        act.wait_ge(S("ts_done"), c_ts)
                        act.activation(TS[u][0:n, :], bank[2 * u][0:n, 0:128], ACT.Copy).then_inc(S("ts_ready"), 1)
                        own(S("ts_ready"))
                    for li, t in enumerate(tiles):
                        c_y0 += 1
                        act.wait_ge(S("gh_done"), c_y0)
                        t0 = TILES[t][0]
                        act.activation(X["y"][:, t0:t0 + n], bank[4 * li][:, 128:128 + n], ACT.Copy).then_inc(S("y0_ready"), 1)
                        own(S("y0_ready"))
                act.wait_ge(S("gvar_done"), p + 1)
                act.activation(X["d"][:, 0:SEQ], bank[7][:, :], ACT.Sqrt, bias=eps_t[:, 1:2], scale=1.0 / 64)
                act.activation(X["d"][:, SEQ:NT], bank[0][:, 0:SAMP], ACT.Sqrt, bias=eps_t[:, 1:2], scale=1.0 / 64
                               ).then_inc(S("gstd_ready"), 1)
                own(S("gstd_ready"))
            for t, (t0, n) in enumerate(TILES):
                act.wait_ge(S("x1_ready"), 6 + t)
                link(act.activation(sqs[0:n, :], x1[0:n, t, :], ACT.Square, accum_out=st[0:n, t, 0:1]))
                act.activation(st[0:n, t, 1:2], st[0:n, t, 0:1], ACT.Sqrt, bias=eps_t[0:n, 0:1], scale=1.0 / D
                               ).then_inc(S("frms_ready"), 1)
                own(S("frms_ready"))
            for t, (t0, n) in enumerate(TILES):
                act.wait_ge(S("xfT_done"), t + 1)
                for half in range(2):
                    ins = act.activation(xfT[:, 4 * half:4 * half + 4, t0:t0 + n],
                                         bank[4 + 2 * (t % 2) + half][:, 0:4 * n].rearrange("p (k n) -> p k n", k=4), ACT.Copy)
                ins.then_inc(S("xfT_ready"), 1)
                own(S("xfT_ready"))
            for j in range(16):
                act.wait_ge(S("qproj_done"), j + 1)
                b = 2 * (j % 2)
                act.activation(qT[:, j, 0:HN], bank[b][:, 0:HN], ACT.Copy)
                act.activation(qT[:, j, HN:NT], bank[b + 1][:, 0:HN], ACT.Copy).then_inc(S("qT_ready"), 1)
            for t, (t0, n) in enumerate(TILES):
                act.wait_ge(S("scores_done"), t + 1)
                for b in range(4):
                    ins = act.activation(sca[0:n, t, 512 * b:512 * b + 512], bank[4 + b][0:n, :], ACT.Copy)
                ins.then_inc(S("scores_ready"), 1)
                own(S("scores_ready"))
            act.activation(xhi[:, :, :], xfT[:, :, :], ACT.Copy).then_inc(S("xhi_ready"), 1)
            act.sem_inc(S("dot_banks_free"), 2)
            act.sem_inc(S("gmat_copied"), 2)
            for q in range(2):
                act.sem_inc(s_act[q], 16)
                act.sem_inc(s_gst[q], 16)

            def split_u(i, step, g):
                act.wait_ge(s_u[g % 2], i * (8 * step) + 16 * (g // 2 + 1))
                act.wait_ge(S("dots_done"), i * (GU * step) + GU * (g + 1))
                act.activation(u_hi[:, g % 2, :, :], u_raw[:, g % 2, :, :], ACT.Copy).then_inc(S("u_hi_ready"), 1)

            def gelu_tile(i, step, g, e):
                q, b = g % 2, 2 * (e % 2)
                if e == 0:
                    act.wait_ge(s_act[q], i * (8 * step) + 16 * (g // 2 + 1))
                act.wait_ge(S("dots_done"), i * (GU * step) + (2 * GU + GU * g + e + 1))
                act.activation(actb[:, q, e, 0:HN], bank[b][:, 0:HN], ACT.Gelu)
                act.activation(actb[:, q, e, HN:NT], bank[b + 1][:, 0:HN], ACT.Gelu).then_inc(S("dot_banks_free"), 1)

            def store_acts(i, step, g):
                act.wait_ge(S("dot_banks_free"), i * (GU * step) + (GU * (g + 1) + 2))
                row = act_d[g // 2] if isinstance(i, int) else act_d[bass.ds(i * (step // 2) + g // 2, 1)].squeeze(0)
                q = g % 2
                act.dma_start(row[:, GU * NT * q:GU * NT * (q + 1)], actb[:, q, :, :].rearrange("p e n -> p (e n)")
                              ).then_inc(s_act[q], 16)

            def shift_exp(t):
                n = TILES[t][1]
                act.wait_ge(S("shifted"), t + 1)
                act.activation(gate[0:n, t, :], gate[0:n, t, :], ACT.Exp).then_inc(S("gexp_ready"), 1)

            def copy_quad(i, t, k):
                o = 4 * (k % 8)
                if k % 8 == 0:
                    act.wait_ge(s_gst[k // 8], i * 16 + 16 * (2 * t + 1))
                act.wait_ge(S("gmat_done"), i * 16 + (32 * t + k + 1))
                act.activation(gst[:, k // 8, :, o:o + 4].rearrange("p a t -> p t a"),
                               bank[5 + k % 2][:, :].rearrange("p (t a) -> p t a", t=4), ACT.Copy
                               ).then_inc(S("gmat_copied"), 1)
                if k % 8 == 7:
                    act.wait_ge(S("gmat_copied"), i * 16 + (2 + 32 * t + k + 1))
                    c = 4 * t + k // 8
                    chunk = gate_d[c] if isinstance(i, int) else gate_d[bass.ds(i * 2 + c, 1)].squeeze(0)
                    act.dma_start(chunk, gst[:, k // 8, :, :]).then_inc(s_gst[k // 8], 16)

            act.wait_ge(s_x1s, 16 * 5)
            act.wait_ge(S("scores_done"), 5)
            act.sem_inc(S("dots_seen"), 1)
            split_u(0, 0, 0)
            for t in range(5):
                with act.Fori(0, PLAIN[t] // 2) as i:
                    for q in range(2):
                        g = PLAIN0[t] + q
                        split_u(i, 2, g + 1)
                        for e in range(GU):
                            gelu_tile(i, 2, g, e)
                        store_acts(i, 2, g)
                shift_exp(t)

                def gated(i, last=False):
                    for j in range(4):
                        g = GATED0[t] + j
                        if not (last and j == 3):
                            split_u(i, 4, g + 1)
                        for e in range(GU):
                            gelu_tile(i, 4, g, e)
                            for k in range(2):
                                copy_quad(i, t, 4 * j + 2 * e + k)
                        store_acts(i, 4, g)

                if t < 4:
                    with act.Fori(0, GATED[t] // 4) as i:
                        gated(i)
                else:
                    gated(0, last=True)
            def split_v(i, g):
                q = g % 2
                act.wait_ge(s_v[q], i * 16 + 16 * (g // 2 + 1))
                act.wait_ge(S("sum_done"), i * 16 + 8 * (g + 1))
                act.activation(v_hi[:, q, :], v_raw[:, q, :], ACT.Copy).then_inc(S("v_hi_ready"), 1)
                act.wait_ge(S("weights_ready"), i * 2 + (g + 1))
                act.activation(w_hi[:, q, :, :], wts[:, q, :, :], ACT.Copy).then_inc(S("w_hi_ready"), 1)

            with act.Fori(0, EG // 2) as i:
                for q in range(2):
                    split_v(i, q)
            for t, (t0, n) in enumerate(TILES):
                act.wait_ge(S("x2_ready"), t + 1)
                link(act.activation(sq_late[0:n, :], x1_late[0:n, t, :], ACT.Square, accum_out=st[0:n, t, 2:3]))
                act.activation(st[0:n, t, 3:4], st[0:n, t, 2:3], ACT.Sqrt, bias=eps_t[0:n, 0:1], scale=1.0 / D
                               ).then_inc(S("yrms_ready"), 1)
                own(S("yrms_ready"))

        @block.tensor
        def _(pe):
            mm = pe.matmul
            pe.wait_ge(s_const, 1)
            for kt in range(KD):
                pe.wait_ge(s_sq, kt + 1)
                mm(bank[0][:, :], ones[:, :], sq[:, kt % 2, 0:SEQ], start=kt == 0, stop=kt == KD - 1)
                mm(bank[1][:, 0:SAMP], ones[:, :], sq[:, kt % 2, SEQ:NT], start=kt == 0, stop=kt == KD - 1
                   ).then_inc(s_sqf, 1)
            pe.wait_ge(s_xn, KD)
            for ji, (kind, p, c0, w, d) in enumerate(JOBS):
                b = 2 * (ji % 2)
                pe.wait_ge(s_w[p % 2], 16 * (p // 2 + 1))
                if ji >= 2:
                    pe.wait_ge(s_pe, ji - 1)
                wp = wbuf[p % 2]
                if kind == "v":
                    t0, n = TILES[d]
                    for kt in range(KD):
                        ins = mm(bank[b][0:n, :], xnT[:, kt, t0:t0 + n], wp[:, kt, 0:w], start=kt == 0, stop=kt == KD - 1)
                else:
                    for kt in range(KD):
                        mm(bank[b][0:w, :], wp[:, kt, c0:c0 + w], xnT[:, kt, 0:SEQ], start=kt == 0, stop=kt == KD - 1)
                        ins = mm(bank[b + 1][0:w, 0:SAMP], wp[:, kt, c0:c0 + w], xnT[:, kt, SEQ:NT],
                                 start=kt == 0, stop=kt == KD - 1)
                ins.then_inc(s_pj, 1)

            def both(b, lhsT, rhs, name):
                b, b2 = b
                mm(bank[b][:, :], lhsT, rhs[:, 0:SEQ], start=True, stop=True)
                mm(bank[b2][:, 0:SAMP], lhsT, rhs[:, SEQ:NT], start=True, stop=True).then_inc(S(name), 1)

            pe.wait_ge(s_const, 2)
            pe.wait_ge(s_pe, NJ)
            pe.wait_ge(S("rows_ready"), 1)
            pe.wait_ge(S("rows_exp"), 1)
            for t, (t0, n) in enumerate(TILES):
                for i, name in enumerate(("Ks", "W")):
                    ins = pe.transpose(bank[4][0:n, 8 * t + 4 * i:8 * t + 4 * i + 4], rows[name][:, t0:t0 + n],
                                       ident[0:4, 0:4])
            ins.then_inc(S("mcol_done"), 1)
            for h in range(MLH):
                if h:
                    pe.wait_ge(S("mix_ready"), h)
                for i, name in enumerate(("E1", "E2", "flo")):
                    if i >= 2:
                        pe.wait_ge(S("bcast_copied"), 3 * h + i - 1)
                    both((2 * (i % 2), 2 * (i % 2) + 1), selr[:, h, :], rows[name], "bcast_done")
                pe.wait_ge(S("qk_ready"), h + 1)
                pe.wait_ge(S("mcol_ready"), 1)
                for t, (t0, n) in enumerate(TILES):
                    dst = bank[4][:, 128 * t:128 * t + 128] if t < PT else bank[5][0:n, 0:128]
                    ins = pe.transpose(dst, kh[:, t0:t0 + n], ident[:, :])
                ins.then_inc(S("ktok_done"), 1)
                for t, (t0, n) in enumerate(TILES):
                    dst = bank[6][:, 128 * t:128 * t + 128] if t < PT else bank[7][0:n, 0:n]
                    ins = mm(dst, kh[:, t0:t0 + n], qh[:, t0:t0 + n], start=True, stop=True)
                ins.then_inc(S("qk_done"), 1)
                pe.wait_ge(S("wv_ready"), h + 1)
                pe.wait_ge(S("ktok_ready"), h + 1)
                pe.wait_ge(S("bcast_copied"), 3 * h + 3)
                for c in range(PT):
                    mm(bank[c // 2][:, 129 * (c % 2):129 * (c % 2) + 129], ktok[:, c, :], wv[:, c, :], start=True, stop=True)
                for b in range(NB):
                    ins = mm(bank[2 + b // 3][:, 129 * (b % 3):129 * (b % 3) + 129], ktok[0:SAMP, PT, :], wvX[:, b, :],
                             start=True, stop=True)
                ins.then_inc(S("upd_done"), 1)
                pe.wait_ge(S("p_ready"), h + 1)
                pe.wait_ge(S("qn_ready"), h + 1)
                for c in range(PT):
                    cs = slice(128 * c, 128 * c + 128)
                    mm(bank[6][:, cs], vaug[:, c, h, 0:128], pmat[:, c, :], start=True, stop=c == 0)
                    if c:
                        mm(bank[6][:, cs], cn[:, c - 1, 0:128], qs[:, cs], start=False, stop=True)
                    mm(bank[7][:, cs], ones[:, :], pmat[:, c, :], start=True, stop=c == 0)
                    if c:
                        mm(bank[7][:, cs], ones[:, :], qn[:, cs], start=False, stop=True)
                mm(bank[5][:, 0:SAMP], vaug[0:SAMP, PT, h, 0:128], pmat[0:SAMP, PT, 0:SAMP], start=True, stop=False,
                   skip_group_check=True)
                for b in range(NB):
                    mm(bank[5][:, 8 * b:8 * b + 8], cn0[:, b, h, 0:128], qs[:, SEQ + 8 * b:SEQ + 8 * b + 8],
                       start=False, stop=True, skip_group_check=True)
                mm(bank[5][:, 64:128], ones[0:SAMP, :], pmat[0:SAMP, PT, 0:SAMP], start=True, stop=False)
                mm(bank[5][:, 64:128], ones[:, :], qn[:, SEQ:NT], start=False, stop=True).then_inc(S("num_done"), 1)
                pe.wait_ge(S("h_ready"), h + 1)
                both((0, 1), ones[:, :], hb, "mean_done")
                pe.wait_ge(S("hsq_ready"), h + 1)
                both((2, 3), ones[:, :], hq, "var_done")
            c_tok = c_u = c_t = c_nv = c_stg = c_pw = c_mg = c_md = c_ts = c_gh = c_st = 0
            for p in range(4):
                pc = slice(128 * p, 128 * p + 128)
                pe.wait_ge(S("lora_act"), 1)
                pe.wait_ge(S("mix_ready"), 4 + p)
                for b, (lhsT, rhs) in enumerate(((w2[:, pc], xwa[0:64, :]), (a2[64:128, pc], xwa[64:128, :]), (g2[:, pc], xg))):
                    mm(bank[2 * b][:, :], lhsT, rhs[:, 0:SEQ], start=True, stop=True)
                    ins = mm(bank[2 * b + 1][:, 0:SAMP], lhsT, rhs[:, SEQ:NT], start=True, stop=True)
                ins.then_inc(S("lora_done"), 1)
                pe.wait_ge(S("kk_squares"), p + 1)
                both((6, 7), blk[:, :], X["t"], "kk_summed")
                pe.wait_ge(S("chan_ready"), p + 1)
                both((0, 1), blk[:, :], X["t"], "bonus_done")
                pe.wait_ge(S("bonus_ready"), p + 1)
                for g, tiles in enumerate(GROUPS):
                    us = units(g)
                    n = TILES[tiles[0]][1]
                    if p or g:
                        pe.wait_ge(S("gh_copied"), c_gh)
                        pe.wait_ge(S("y0_ready"), c_gh)
                    for li, t in enumerate(tiles):
                        t0 = TILES[t][0]
                        for a, src in enumerate((AR[:, 0, :], X["be"], X["ka"], X["v"])):
                            ins = pe.transpose(bank[4 * li + 3][0:n, 128 * a:128 * a + 128], src[:, t0:t0 + n], ident[:, :])
                        ins.then_inc(S("tok_done"), 1)
                    for u, (t, h) in enumerate(us):
                        t0 = TILES[t][0]
                        hs, ts_ = slice(64 * h, 64 * h + 64), slice(t0, t0 + n)
                        for a, key in enumerate((X["be"], X["ka"])):
                            ins = mm(bank[2 * u][0:n, 2 * a * n:2 * (a + 1) * n], key[hs, ts_], AR[hs, :, ts_],
                                     start=True, stop=True)
                        ins.then_inc(S("gram_done"), 1)
                    c_tok += len(tiles)
                    pe.wait_ge(S("tok_ready"), c_tok)
                    for u, (t, h) in enumerate(us):
                        t0 = TILES[t][0]
                        hs, ts_ = slice(64 * h, 64 * h + 64), slice(t0, t0 + n)
                        mm(bank[2 * u + 1][0:n, 0:n], AR[hs, 0, ts_], X["be"][hs, ts_], start=True, stop=True
                           ).then_inc(S("m_done"), 1)
                    for u, (t, h) in enumerate(us):
                        pe.wait_ge(S("masked"), (c_u := c_u + 1))
                        mm(bank[2 * u + 1][0:n, 0:64], G4[u][0:n, 2, 0:n], tok4[0:n, u // 2, 3, 64 * h:64 * h + 64],
                           start=True, stop=True).then_inc(S("nv_done"), 1)
                    nst = 4 if n == 128 else 3
                    for s in range(nst):
                        for u in range(len(us)):
                            if s == 0:
                                M, MT = M3[u][0:n, 0, 0:n], G4[u][0:n, 0, 0:n]
                                mm(bank[2 * u][0:n, 0:n], MT, M, start=True, stop=True)
                                ins = mm(bank[2 * u][0:n, n:2 * n], M, MT, start=True, stop=True)
                            else:
                                c_pw += 1
                                pe.wait_ge(S("powers_ready"), c_pw)
                                pe.wait_ge(S("inverse_step"), c_stg - len(us) + 1)
                                old = XM[u][(s - 1) % 2]
                                if s < nst - 1:
                                    mm(bank[2 * u][0:n, 0:n], old[0:n, 1, 0:n], old[0:n, 0, 0:n], start=True, stop=True)
                                    ins = mm(bank[2 * u][0:n, n:3 * n], old[0:n, 0, 0:n], old[0:n, 1:3, 0:n],
                                             start=True, stop=True)
                                else:
                                    ins = mm(bank[2 * u][0:n, 2 * n:3 * n], old[0:n, 0, 0:n], old[0:n, 2, 0:n],
                                             start=True, stop=True)
                            ins.then_inc(S("stage_done"), 1)
                            c_stg += 1
                    c_md_step = c_stg - len(us)
                    R = [XM[u][(nst - 1) % 2] for u in range(len(us))]
                    if n == 128:
                        for m in range(2):
                            for u in range(len(us)):
                                if m == 0:
                                    pe.wait_ge(S("inverse_step"), c_stg - len(us) + u + 1)
                                else:
                                    pe.wait_ge(S("merged"), c_md - len(us) + u + 1)
                                r = XM[u][(nst - 1 + m) % 2][:, 2, :]
                                pe.transpose(bank[2 * u][:, 0:128], r, ident[:, :])
                                mm(bank[2 * u][:, 128:256], M3[u][:, 1 + m, :], r, start=True, stop=True
                                   ).then_inc(S("merge_a"), 1)
                            for u in range(len(us)):
                                c_mg += 1
                                pe.wait_ge(S("merge_b"), c_mg)
                                if m == 0:
                                    pe.wait_ge(S("nv_ready"), c_nv + u + 1)
                                mm(bank[2 * u + 1][:, 0:128], TB[u][:, 0, :], TB[u][:, 1, :], start=True, stop=True
                                   ).then_inc(S("merge_c"), 1)
                                c_md += 1
                        R = [XM[u][(nst + 1) % 2] for u in range(len(us))]
                    for u, (t, h) in enumerate(us):
                        if n == 128:
                            pe.wait_ge(S("merged"), c_md - len(us) + u + 1)
                        else:
                            pe.wait_ge(S("inverse_step"), c_stg - len(us) + u + 1)
                        pe.wait_ge(S("nv_ready"), c_nv + u + 1)
                        mm(bank[2 * u][0:n, 0:64], R[u][0:n, 2, 0:n], tok4[0:n, u // 2, 0, 64 * h:64 * h + 64],
                           start=True, stop=True)
                        mm(bank[2 * u][0:n, 64:128], R[u][0:n, 2, 0:n], NV[u][0:n, :], start=True, stop=True
                           ).then_inc(S("ts_done"), 1)
                    c_nv += len(us)
                    if n < 128:
                        pe.wait_ge(S("spread"), p + 1)
                    for li, t in enumerate(tiles):
                        for h in range(2):
                            u = 2 * li + h
                            c_ts += 1
                            pe.wait_ge(S("ts_ready"), c_ts)
                        for h in range(2):
                            u = 2 * li + h
                            hs = slice(64 * h, 64 * h + 64)
                            ta, sa = TS[u][0:n, 0:64], TS[u][0:n, 64:128]
                            tk = tok4[0:n, li, :, hs]
                            ru, rv, rw = bank[4 * li], bank[4 * li + 1], bank[4 * li + 3]
                            mm(ru[hs, 0:n], ta, G4[u][0:n, 1, 0:n], start=True, stop=True)
                            mm(ru[hs, 128:128 + n], sa, G4[u][0:n, 1, 0:n], start=True, stop=False)
                            mm(ru[hs, 128:128 + n], tk[:, 3, :], G4[u][0:n, 3, 0:n], start=False, stop=True)
                            if n == 128:
                                for c in range(2):
                                    cs, dst = slice(64 * c, 64 * c + 64), (rv, rw)[c]
                                    mm(dst[hs, 0:64], ta[cs, :], tk[cs, 1, :], start=True, stop=True)
                                    mm(dst[hs, 64:128], tk[cs, 1, :], sa[cs, :], start=True, stop=False)
                                    ins = mm(dst[hs, 64:128], tk[cs, 2, :], tk[cs, 3, :], start=False, stop=True)
                            else:
                                mm(rv[hs, :], ta, bX[:, :, hs], start=True, stop=True)
                                for c in range(NB):
                                    mm(rw[hs, 64 * c:64 * c + 64], bX[:, c, hs], sa, start=True, stop=False)
                                    ins = mm(rw[hs, 64 * c:64 * c + 64], kX[:, c, hs], tk[:, 3, :], start=False, stop=True)
                        ins.then_inc(S("gh_done"), 1)
                        c_gh += 1
                pe.wait_ge(S("gh_copied"), c_gh)
                pe.wait_ge(S("y0_ready"), c_gh)
                for b in range(NB):
                    for h in range(2):
                        hs = slice(64 * h, 64 * h + 64)
                        ins = mm(bank[2][hs, 64 * b:64 * b + 64], GtS[hs, b, :], s0[hs, b, p, :], start=True, stop=True)
                ins.then_inc(S("sstep_done"), 1)
                for c in range(1, 8):
                    c_st += 1
                    pe.wait_ge(S("state_ready"), c_st + p)
                    for h in range(2):
                        hs = slice(64 * h, 64 * h + 64)
                        ins = mm(bank[c % 2][hs, 0:64], Gt[hs, c, :], Sst[hs, c - 1, :], start=True, stop=True)
                    ins.then_inc(S("state_step"), 1)
                for c in range(1, 8):
                    for h in range(2):
                        hs = slice(64 * h, 64 * h + 64)
                        cs = slice(64 * c, 64 * c + 64)
                        mm(bank[3][hs, cs], Sst[hs, c - 1, :], X["reff"][hs, cs], start=True, stop=True)
                for b in range(NB):
                    for h in range(2):
                        hs = slice(64 * h, 64 * h + 64)
                        ins = mm(bank[4][hs, 8 * b:8 * b + 8], s0[hs, b, p, :], X["reff"][hs, SEQ + 8 * b:SEQ + 8 * b + 8],
                                 start=True, stop=True)
                ins.then_inc(S("y_inter"), 1)
                pe.wait_ge(S("y_full"), p + 1)
                both((5, 6), blk[:, :], X["y"], "gmean_done")
                pe.wait_ge(S("gsq_ready"), p + 1)
                both((7, 0), blk[:, :], X["kk"], "gvar_done")
            pe.wait_ge(S("mix_ready"), 8)
            for half in range(2):
                pe.wait_ge(s_ring[half], 16)
                for t, (t0, n) in enumerate(TILES):
                    jj = 5 * half + t
                    if jj >= 4:
                        pe.wait_ge(S("x1_ready"), jj - 3)
                    for kt in range(KD):
                        ins = mm(bank[jj % 4][0:n, :], mixT[:, kt, t0:t0 + n], wring[:, half, kt, :], start=kt == 0,
                                 stop=kt == KD - 1)
                    ins.then_inc(S("outproj_done"), 1)
            for t, (t0, n) in enumerate(TILES):
                pe.wait_ge(S("xf_ready"), t + 1)
                if t >= 2:
                    pe.wait_ge(S("xfT_ready"), t - 1)
                for kt in range(KD):
                    ins = pe.transpose(bank[4 + 2 * (t % 2) + kt // 4][:, n * (kt % 4):n * (kt % 4) + n],
                                       xf[0:n, t % 2, 128 * kt:128 * kt + 128], ident[0:n, 0:n])
                ins.then_inc(S("xfT_done"), 1)
            pe.wait_ge(S("xfT_ready"), 5)
            pe.wait_ge(S("x1_ready"), 10)
            for j in range(16):
                pp = j // 4
                pe.wait_ge(s_ring[pp % 2], 16 * (pp // 2 + 2))
                if j >= 2:
                    pe.wait_ge(S("qT_ready"), j - 1)
                b = 2 * (j % 2)
                for kt in range(KD):
                    lhsT = wring[:, pp % 2, kt, 128 * (j % 4):128 * (j % 4) + 128]
                    mm(bank[b][:, 0:HN], lhsT, xfT[:, kt, 0:HN], start=kt == 0, stop=kt == KD - 1)
                    ins = mm(bank[b + 1][:, 0:HN], lhsT, xfT[:, kt, HN:NT], start=kt == 0, stop=kt == KD - 1)
                ins.then_inc(S("qproj_done"), 1)
            pe.wait_ge(S("qT_ready"), 16)
            pe.wait_ge(s_sub, 16)
            for t, (t0, n) in enumerate(TILES):
                if t:
                    pe.wait_ge(S("scores_ready"), t)
                for j in range(16):
                    ins = mm(bank[4 + j // 4][0:n, 128 * (j % 4):128 * (j % 4) + 128], qT[:, j, t0:t0 + n], subT[:, j, :],
                             start=True, stop=True)
                ins.then_inc(S("scores_done"), 1)
            pe.wait_ge(S("scores_ready"), 5)

            def dots(i, step, g, e):
                q, b = g % 2, 2 * (e % 2)
                if e == 0:
                    pe.wait_ge(S("u_lo_ready"), i * step + (g + 1))
                pe.wait_ge(S("dot_banks_free"), i * (GU * step) + (GU * g + e + 1))
                es = slice(128 * e, 128 * e + 128)
                for kt in range(KD):
                    hi, lo = u_hi[:, q, kt, es], u_lo[:, q, kt, es]
                    xh, xl = xhi[:, kt, :], xlo[:, kt, :]
                    for m, (lhsT, rhs) in enumerate(((hi, xh), (hi, xl), (lo, xh))):
                        on = dict(start=kt == 0 and m == 0, stop=kt == KD - 1 and m == 2)
                        mm(bank[b][:, 0:HN], lhsT, rhs[:, 0:HN], **on)
                        ins = mm(bank[b + 1][:, 0:HN], lhsT, rhs[:, HN:NT], **on)
                ins.then_inc(S("dots_done"), 1)

            def gate_quad(i, t, k):
                pe.wait_ge(S("hot_a_ready"), i * 16 + (32 * t + k + 1))
                pe.wait_ge(S("hot_b_ready"), i * 16 + (32 * t + k + 1))
                pe.wait_ge(S("gmat_copied"), i * 16 + (32 * t + k + 1))
                for j in range(4):
                    slot = (4 * k + j) % 8
                    for part in range(2):
                        ins = mm(bank[5 + k % 2][:, 128 * j:128 * j + 128], hot_b[:, slot, :], hot_a[:, part, slot, :],
                                 start=part == 0, stop=part == 1)
                ins.then_inc(S("gmat_done"), 1)

            pe.sem_inc(S("dots_done"), 2 * GU)
            pe.wait_ge(S("xlo_ready"), 1)
            for t, (t0, n) in enumerate(TILES):
                with pe.Fori(0, PLAIN[t] // 2) as i:
                    for q in range(2):
                        for e in range(GU):
                            dots(i, 2, PLAIN0[t] + q, e)
                pe.wait_ge(S("routed"), t + 1)
                for a, src in enumerate((isel[0:n, 0, :], isel[0:n, 1, :], gate[0:n, t, :])):
                    ins = pe.transpose(bank[4][:, n * a:n * a + n], src, ident[0:n, 0:n])
                ins.then_inc(S("hk_done"), 1)

                def gated(i):
                    for j in range(4):
                        for e in range(GU):
                            dots(i, 4, GATED0[t] + j, e)
                            for k in range(2):
                                gate_quad(i, t, 4 * j + 2 * e + k)

                if t < 4:
                    with pe.Fori(0, GATED[t] // 4) as i:
                        gated(i)
                else:
                    gated(0)
            pe.sem_inc(S("sum_done"), 2 * KD)
            pe.wait_ge(S("dot_banks_free"), GU * UG + 2)
            pe.wait_ge(S("gmat_copied"), NT // 4 + 2)
            with pe.Fori(0, EG // 2) as i:
                for q in range(2):
                    pe.wait_ge(S("w_lo_ready"), i * 2 + (q + 1))
                    pe.wait_ge(S("v_lo_ready"), i * 2 + (q + 1))
                    for c in range(KD):
                        b = 2 * (c % 4)
                        pe.wait_ge(S("sum_banks_free"), i * 16 + (8 * q + c + 1))
                        for e in range(GE):
                            vs = slice(D * e + 128 * c, D * e + 128 * c + 128)
                            hi, lo = v_hi[:, q, vs], v_lo[:, q, vs]
                            for m, (lhsT, rhs) in enumerate(((hi, w_hi), (hi, w_lo), (lo, w_hi))):
                                on = dict(start=e == 0 and m == 0, stop=e == GE - 1 and m == 2)
                                mm(bank[b][:, 0:HN], lhsT, rhs[:, q, e, 0:HN], **on)
                                ins = mm(bank[b + 1][:, 0:HN], lhsT, rhs[:, q, e, HN:NT], **on)
                        ins.then_inc(S("sum_done"), 1)
            pe.wait_ge(S("sum_banks_free"), 4 + 8 * EG)
            for t, (t0, n) in enumerate(TILES):
                if t >= 4:
                    pe.wait_ge(S("x2_ready"), t - 3)
                for kt in range(KD):
                    ins = pe.transpose(bank[2 * (t % 4) + kt // 4][0:n, 128 * (kt % 4):128 * (kt % 4) + 128],
                                       acc[:, kt, t0:t0 + n], ident[:, :])
                ins.then_inc(S("back_done"), 1)

        @block.vector
        def _(dve):
            k = [0]

            def link(ins):
                k[0] += 1
                ins.then_inc(c_dve, 1)
                dve.wait_ge(c_dve, k[0])

            raised = {}

            def own(signal):
                raised[signal.name] = raised.get(signal.name, 0) + 1
                dve.wait_ge(signal, raised[signal.name])

            TT, TS_, STT = dve.tensor_tensor, dve.tensor_scalar, dve.scalar_tensor_tensor

            def seqs(ap, lead):
                return ap[:, lead + SEQ:].rearrange("p (b s) -> p b s", b=NB)

            def steps(ap):
                return ap.rearrange("p (b s) -> p b s", b=NB)

            dve.wait_ge(s_par, 16)
            dve.wait_ge(s_sd, 2)
            link(dve.reciprocal(rb[:, :], rb[:, :]))
            for kt in range(KD):
                STT(out=xnT[:, kt, :], in0=xnT[:, kt, :], scalar=pcol("g_mix", kt), in1=rb[:, :], op0=ALU.mult,
                    op1=ALU.mult).then_inc(s_xn, 1)
                own(s_xn)
            dve.wait_ge(s_init, 16 * 8)
            link(dve.tensor_copy(ext_q[:, :, 3 + SEQ:].rearrange("p c (b s) -> p c b s", b=NB)[:, :, :, 0:3], conv0[:, :, :, :]))
            link(dve.tensor_copy(ext_r[:, :, 1 + SEQ:].rearrange("p c (b s) -> p c b s", b=NB)[:, :, :, 0], shift0[:, :, :]))
            dve.wait_ge(s_const, 2)
            dve.wait_ge(s_pe, NJ)
            r = rows
            STT(out=r["l"][:, :], in0=gf[:, :], scalar=-1.0, in1=gf[:, :], op0=ALU.mult, op1=ALU.max).then_inc(S("gate_abs"), 1)
            own(S("gate_abs"))
            link(TS_(gf[:, :], gf[:, :], 0.0, None, ALU.min))
            dve.wait_ge(S("gate_log"), 1)
            link(TT(gf[:, :], gf[:, :], r["l"][:, :], ALU.subtract))
            link(dve.tensor_tensor_scan(r["b"][:, :], rst_m[:, :], gf[:, :], 0.0, ALU.mult, ALU.add))
            link(dve.tensor_tensor_scan(r["m"][:, 0:SEQ], gf[:, 0:SEQ], gi[:, 0:SEQ], NEG, ALU.add, ALU.max))
            for b in range(NB):
                s = slice(SEQ + NS * b, SEQ + NS * b + NS)
                link(dve.tensor_tensor_scan(r["m"][:, s], gf[:, s], gi[:, s], small[:, 2 + b:3 + b], ALU.add, ALU.max))
            link(TT(r["E1"][:, :], r["b"][:, :], r["m"][:, :], ALU.subtract))
            link(TT(r["Ks"][:, :], gi[:, :], r["b"][:, :], ALU.subtract))
            link(TS_(r["E2"][:, 0:MCH], r["E1"][:, 0:MCH], NEG, None, ALU.add))
            for c in range(1, PT):
                s = slice(MCH * c, MCH * c + MCH)
                link(TS_(r["E2"][:, s], r["E1"][:, s], r["m"][:, MCH * c - 1:MCH * c], None, ALU.add))
            for b in range(NB):
                s = slice(SEQ + NS * b, SEQ + NS * b + NS)
                link(TS_(r["E2"][:, s], r["E1"][:, s], small[:, 2 + b:3 + b], None, ALU.add))
            for lo, hi, w in ((0, SEQ, MCH), (SEQ, NT, NS)):
                v = [r[n][:, lo:hi].rearrange("p (c w) -> p c w", w=w) for n in ("W", "Ks", "E1")]
                last = TT(v[0], v[1], v[2][:, :, w - 1:w].to_broadcast([4, (hi - lo) // w, w]), ALU.add)
                if lo == 0:
                    link(last)
            last.then_inc(S("rows_ready"), 1)
            own(S("rows_ready"))
            link(dve.tensor_copy(mo[:, 0:1], r["m"][:, SEQ - 1:SEQ]))
            dve.tensor_copy(mo[:, 1:], r["m"][:, SEQ + NS - 1:NT:NS]).then_inc(S("m_ready"), 1)
            own(S("m_ready"))
            dve.wait_ge(S("mcol_done"), 1)
            link(dve.tensor_copy(mcol[:, 0:PT, :, :], bank[4][:, 0:8 * PT].rearrange("p (t a h) -> p t a h", t=PT, a=2)))
            link(dve.tensor_copy(mcol[0:SAMP, PT, :, :], bank[4][0:SAMP, 8 * PT:8 * PT + 8].rearrange("p (a h) -> p a h", a=2)))
            for h in range(MLH):
                last = TS_(wcolX[:, h, :], seqm[:, :], mcol[0:SAMP, PT, 1, h:h + 1], None, ALU.mult)
            last.then_inc(S("mcol_ready"), 1)
            own(S("mcol_ready"))
            dve.wait_ge(S("mcol_ready"), 1)
            for h in range(MLH):
                for i, ct in enumerate((h, 4 + h)):
                    for part in range(2):
                        for j in range(CW):
                            if part == 0:
                                src, dst = ext_q[:, ct, j:j + SEQ], pre[:, i, 0:SEQ]
                            else:
                                src, dst = seqs(ext_q[:, ct, :], 3)[:, :, j:j + NS], steps(pre[:, i, SEQ:NT])
                            w = pcol("conv_w", 8 * j + ct)
                            if j == 0:
                                link(TS_(dst, src, w, pcol("conv_b", ct), ALU.mult, ALU.add))
                            else:
                                last = STT(out=dst, in0=src, scalar=w, in1=dst, op0=ALU.mult, op1=ALU.add)
                                if part == 0 or j < CW - 1:
                                    link(last)
                    last.then_inc(S("conv_ready"), 1)
                    own(S("conv_ready"))
                dve.wait_ge(S("conv_sig"), 2 * h + 2)
                link(TT(qh[:, :], pre[:, 0, :], sg[:, 0, :], ALU.mult))
                STT(out=kh[:, :], in0=pre[:, 1, :], scalar=128 ** -0.5, in1=sg[:, 1, :], op0=ALU.mult, op1=ALU.mult
                    ).then_inc(S("qk_ready"), 1)
                own(S("qk_ready"))
                dve.wait_ge(S("bcast_copied"), 3 * h + 3)
                link(TT(qs[:, :], qh[:, :], bc[:, 1, :], ALU.mult))
                for t, (t0, n) in enumerate(TILES):
                    last = STT(out=dmat[0:n, t, 0:n], in0=bc[0:n, 0, t0:t0 + n], scalar=mcol[0:n, t, 0, h:h + 1],
                               in1=negm[:, :] if t < PT else negs[:, :], op0=ALU.add, op1=ALU.add)
                last.then_inc(S("dlog_ready"), 1)
                own(S("dlog_ready"))
                for c in range(PT):
                    TS_(wv[:, c, :], vaug[:, c, h, :], mcol[:, c, 1, h:h + 1], None, ALU.mult)
                for b in range(NB):
                    last = TS_(wvX[:, b, :], vaug[0:SAMP, PT, h, :], wcolX[:, h, b:b + 1], None, ALU.mult)
                last.then_inc(S("wv_ready"), 1)
                own(S("wv_ready"))
                dve.wait_ge(S("qk_done"), h + 1)
                dve.wait_ge(S("d_ready"), h + 1)
                link(TT(pmat[:, 0:PT, :], bank[6][:, :].rearrange("p (t n) -> p t n", t=PT), dmat[:, 0:PT, :], ALU.mult))
                TT(pmat[0:SAMP, PT, 0:SAMP], bank[7][0:SAMP, 0:SAMP], dmat[0:SAMP, PT, 0:SAMP], ALU.mult).then_inc(S("p_ready"), 1)
                own(S("p_ready"))
                dve.wait_ge(S("upd_done"), h + 1)
                if h:
                    dve.wait_ge(s_out, 16 * (1 + 2 * h))
                link(dve.tensor_copy(cn[:, 0, :], bank[0][:, 0:129]))
                for c in range(1, PT):
                    link(STT(out=cn[:, c, :], in0=cn[:, c - 1, :], scalar=bc[:, 1, MCH * (c + 1) - 1:MCH * (c + 1)],
                             in1=bank[c // 2][:, 129 * (c % 2):129 * (c % 2) + 129], op0=ALU.mult, op1=ALU.add))
                for b in range(NB):
                    e = SEQ + NS * (b + 1)
                    last = STT(out=cnS[:, b, :], in0=cn0[:, b, h, :], scalar=bc[:, 1, e - 1:e],
                               in1=bank[2 + b // 3][:, 129 * (b % 3):129 * (b % 3) + 129], op0=ALU.mult, op1=ALU.add)
                last.then_inc(S("cn_ready"), 1)
                own(S("cn_ready"))
                for c in range(1, PT):
                    s = slice(MCH * c, MCH * c + MCH)
                    TS_(qn[:, s], qs[:, s], cn[:, c - 1, 128:129], None, ALU.mult)
                TT(steps(qn[:, SEQ:NT]), steps(qs[:, SEQ:NT]), cn0[:, :, h, 128:129].to_broadcast([128, NB, NS]), ALU.mult
                   ).then_inc(S("qn_ready"), 1)
                own(S("qn_ready"))
                dve.wait_ge(S("num_done"), h + 1)
                for dst, den, fl in ((hr[:, 0:SEQ], bank[7][:, :], bc[:, 2, 0:SEQ]), (hr[:, SEQ:NT], bank[5][:, 64:128], bc[:, 2, SEQ:NT])):
                    link(STT(out=dst, in0=den, scalar=-1.0, in1=fl, op0=ALU.mult, op1=ALU.max))
                    link(TT(dst, den, dst, ALU.max))
                link(dve.reciprocal(hr[:, :], hr[:, :]))
                link(TT(hb[:, 0:SEQ], bank[6][:, :], hr[:, 0:SEQ], ALU.mult))
                TT(hb[:, SEQ:NT], bank[5][:, 0:SAMP], hr[:, SEQ:NT], ALU.mult).then_inc(S("h_ready"), 1)
                own(S("h_ready"))
                dve.wait_ge(S("mean_done"), h + 1)
                dve.wait_ge(S("h_ready"), h + 1)
                for dst, src in zip(main_samp(hb), (bank[0][:, :], bank[1][:, 0:SAMP])):
                    link(STT(out=dst, in0=src, scalar=-1.0 / 128, in1=dst, op0=ALU.mult, op1=ALU.add))
                TT(hq[:, :], hb[:, :], hb[:, :], ALU.mult).then_inc(S("hsq_ready"), 1)
                own(S("hsq_ready"))
                dve.wait_ge(S("std_ready"), h + 1)
                link(dve.reciprocal(hr[:, :], hr[:, :]))
                link(STT(out=hb[:, :], in0=hb[:, :], scalar=pcol("ml_g", h), in1=hr[:, :], op0=ALU.mult, op1=ALU.mult))
                TT(mixT[:, h, :], hb[:, :], osig[:, h, :], ALU.mult).then_inc(S("mix_ready"), 1)
                own(S("mix_ready"))
            eq = ext_q[:, :, 3 + SEQ:].rearrange("p c (b s) -> p c b s", b=NB)
            er = ext_r[:, :, 1 + SEQ:].rearrange("p c (b s) -> p c b s", b=NB)
            link(dve.tensor_copy(conv_t[:, :, 0, :], ext_q[:, :, SEQ:SEQ + 3]))
            dve.tensor_copy(conv_t[:, :, 1:, :], eq[:, :, :, NS:NS + 3]).then_inc(S("tails_ready"), 1)
            own(S("tails_ready"))
            link(dve.tensor_copy(shift_t[:, :, 0], ext_r[:, :, SEQ]))
            dve.tensor_copy(shift_t[:, :, 1:], er[:, :, :, NS]).then_inc(S("tails_ready"), 1)
            own(S("tails_ready"))
            dve.wait_ge(s_out, 16 * 11)
            dve.wait_ge(S("mix_ready"), 4)

            def shifted(dst, ct):
                for part in range(2):
                    if part == 0:
                        cur, prev = ext_r[:, ct, 1:1 + SEQ], ext_r[:, ct, 0:SEQ]
                        d, o = X["d"][:, 0:SEQ], dst[:, 0:SEQ]
                    else:
                        e = seqs(ext_r[:, ct, :], 1)
                        cur, prev = e[:, :, 1:], e[:, :, 0:NS]
                        d, o = steps(X["d"][:, SEQ:NT]), steps(dst[:, SEQ:NT])
                    link(TT(d, prev, cur, ALU.subtract))
                    last = STT(out=o, in0=d, scalar=pcol("mu", ct), in1=cur, op0=ALU.mult, op1=ALU.add)
                    if part == 0:
                        link(last)
                return last

            link(shifted(xwa, 12))
            shifted(xg, 13).then_inc(S("lora_in"), 1)
            own(S("lora_in"))
            c_u = c_stg = c_md = c_gh = c_st = c_tok = c_pw = 0
            for p in range(4):
                link(shifted(X["r"], p))
                link(shifted(X["k"], 4 + p))
                link(shifted(X["v"], 8 + p))
                link(TS_(X["kk"][:, :], X["k"][:, :], pcol("k_k", p), None, ALU.mult))
                TT(X["t"][:, :], X["kk"][:, :], X["kk"][:, :], ALU.mult).then_inc(S("kk_squares"), 1)
                own(S("kk_squares"))
                dve.wait_ge(S("kk_summed"), p + 1)
                for dst, src in zip(main_samp(X["t"]), (bank[6][:, :], bank[7][:, 0:SAMP])):
                    last = TS_(dst, src, 1e-24, None, ALU.max)
                last.then_inc(S("kk_clamped"), 1)
                own(S("kk_clamped"))
                dve.wait_ge(S("lora_out"), p + 1)
                link(TS_(X["sw"][:, :], X["sw"][:, :], -math.exp(-0.5), None, ALU.mult))
                link(dve.tensor_tensor_scan(X["cum"][:, :], rst_r[:, :], X["sw"][:, :], 0.0, ALU.mult, ALU.add))
                TT(X["cm"][:, :], X["cum"][:, :], X["sw"][:, :], ALU.subtract).then_inc(S("cum_ready"), 1)
                own(S("cum_ready"))
                dve.wait_ge(S("kk_norm"), p + 1)
                link(dve.reciprocal(X["t"][:, :], X["t"][:, :]))
                link(TT(X["kk"][:, :], X["kk"][:, :], X["t"][:, :], ALU.mult))
                link(TS_(X["t"][:, :], X["av"][:, :], 1.0, pcol("k_a", p), ALU.subtract, ALU.mult))
                link(STT(out=X["kf"][:, :], in0=X["t"][:, :], scalar=1.0, in1=X["k"][:, :], op0=ALU.add, op1=ALU.mult))
                link(TT(X["be"][:, :], X["kk"][:, :], X["av"][:, :], ALU.mult))
                dve.wait_ge(S("decay_ready"), p + 1)
                link(TT(X["be"][:, :], X["be"][:, :], X["En"][:, :], ALU.mult))
                link(STT(out=AR[:, 0, :], in0=X["kk"][:, :], scalar=-1.0, in1=X["cm"][:, :], op0=ALU.mult, op1=ALU.mult))
                link(TT(AR[:, 1, :], X["r"][:, :], X["Ep"][:, :], ALU.mult))
                link(TT(X["ka"][:, :], X["kf"][:, :], X["En"][:, :], ALU.mult))
                STT(out=X["t"][:, :], in0=X["r"][:, :], scalar=pcol("r_k", p), in1=X["kf"][:, :], op0=ALU.mult,
                    op1=ALU.mult).then_inc(S("chan_ready"), 1)
                own(S("chan_ready"))
                dve.wait_ge(S("bonus_done"), p + 1)
                for dst, src, v in zip(main_samp(X["bv"]), (bank[0][:, :], bank[1][:, 0:SAMP]), main_samp(X["v"])):
                    last = TT(dst, src, v, ALU.mult)
                last.then_inc(S("bonus_ready"), 1)
                own(S("bonus_ready"))
                for g, tiles in enumerate(GROUPS):
                    us = units(g)
                    n = TILES[tiles[0]][1]
                    m4, m3 = (mask4[:, :, :], mask3[:, :, :]) if n == 128 else (mask4s[:, :, :], masks[:, :])
                    for u in range(len(us)):
                        dve.wait_ge(S("gram_done"), c_u + u + 1)
                        link(TT(G4[u][0:n, :, 0:n], bank[2 * u][0:n, 0:4 * n].rearrange("p (a n) -> p a n", a=4), m4, ALU.mult))
                    for u in range(len(us)):
                        c_u += 1
                        dve.wait_ge(S("m_done"), c_u)
                        src = bank[2 * u + 1][0:n, 0:n]
                        if n == 128:
                            TT(M3[u][:, :, :], src.unsqueeze(1).to_broadcast([128, 3, 128]), m3, ALU.mult).then_inc(S("masked"), 1)
                            own(S("masked"))
                        else:
                            TT(M3[u][0:n, 0, 0:n], src, m3, ALU.mult).then_inc(S("masked"), 1)
                            own(S("masked"))
                    c_tok += len(tiles)
                    if n < 128:
                        dve.wait_ge(S("tok_ready"), c_tok)
                        link(TT(bX[:, :, :], tok4[0:n, 0, 1, :].unsqueeze(1).to_broadcast([n, NB, 128]),
                                seqm[:, :].unsqueeze(2).to_broadcast([n, NB, 128]), ALU.mult))
                        TT(kX[:, :, :], tok4[0:n, 0, 2, :].unsqueeze(1).to_broadcast([n, NB, 128]),
                           seqm[:, :].unsqueeze(2).to_broadcast([n, NB, 128]), ALU.mult).then_inc(S("spread"), 1)
                        own(S("spread"))
                    nst = 4 if n == 128 else 3
                    for s in range(nst):
                        for u in range(len(us)):
                            c_stg += 1
                            if s == 0:
                                TT(XM[u][0][0:n, 2, 0:n], G4[u][0:n, 0, 0:n], ident[0:n, 0:n], ALU.add
                                   ).then_inc(S("inverse_step"), 1)
                                own(S("inverse_step"))
                            else:
                                dve.wait_ge(S("stage_done"), c_stg)
                                dve.wait_ge(S("powers_ready"), c_pw + min(len(us) * s + u + 1, len(us) * (nst - 1)))
                                dve.wait_ge(S("inverse_step"), c_stg - len(us))
                                TT(XM[u][s % 2][0:n, 2, 0:n], bank[2 * u][0:n, 2 * n:3 * n], XM[u][(s - 1) % 2][0:n, 2, 0:n],
                                   ALU.add).then_inc(S("inverse_step"), 1)
                                own(S("inverse_step"))
                    c_pw += len(us) * (nst - 1)
                    if n == 128:
                        for m in range(2):
                            for u in range(len(us)):
                                c_md += 1
                                dve.wait_ge(S("merge_c"), c_md)
                                if m == 0:
                                    dve.wait_ge(S("inverse_step"), c_stg)
                                else:
                                    dve.wait_ge(S("merged"), c_md - len(us))
                                TT(XM[u][(nst + m) % 2][:, 2, :], bank[2 * u + 1][:, 0:128], XM[u][(nst - 1 + m) % 2][:, 2, :],
                                   ALU.add).then_inc(S("merged"), 1)
                                own(S("merged"))
                    for li, t in enumerate(tiles):
                        t0 = TILES[t][0]
                        c_gh += 1
                        dve.wait_ge(S("gh_done"), c_gh)
                        dve.wait_ge(S("y0_ready"), c_gh)
                        TT(X["reff"][:, t0:t0 + n], bank[4 * li][:, 0:n], AR[:, 1, t0:t0 + n], ALU.add)
                        rv, rw = bank[4 * li + 1], bank[4 * li + 3]
                        if n == 128:
                            for c in range(2):
                                e, src = t0 + RCH * (c + 1), (rv, rw)[c]
                                TT(Gt[:, 2 * t + c, :], src[:, 0:64], id64[:, :], ALU.add)
                                last = TS_(PH[:, 2 * t + c, :], src[:, 64:128], X["Ep"][:, e - 1:e], None, ALU.mult)
                        else:
                            TT(GtS[:, :, :], rv[:, :].rearrange("p (c d) -> p c d", c=NB),
                               id64[:, :].unsqueeze(1).to_broadcast([128, NB, 64]), ALU.add)
                            last = TT(PHS[:, :, :], rw[:, :].rearrange("p (c d) -> p c d", c=NB),
                                      X["Ep"][:, SEQ + NS - 1:NT:NS].unsqueeze(2).to_broadcast([128, NB, 64]), ALU.mult)
                        last.then_inc(S("gh_copied"), 1)
                        own(S("gh_copied"))
                dve.wait_ge(S("gh_copied"), c_gh)
                if p:
                    dve.wait_ge(s_out, 16 * (11 + 2 * p))
                dve.tensor_copy(Sst[:, 0, :], PH[:, 0, :]).then_inc(S("state_ready"), 1)
                own(S("state_ready"))
                for c in range(1, 8):
                    c_st += 1
                    e = RCH * (c + 1)
                    dve.wait_ge(S("state_step"), c_st)
                    STT(out=Sst[:, c, :], in0=bank[c % 2][:, 0:64], scalar=X["Ep"][:, e - 1:e], in1=PH[:, c, :],
                        op0=ALU.mult, op1=ALU.add).then_inc(S("state_ready"), 1)
                    own(S("state_ready"))
                dve.wait_ge(S("sstep_done"), p + 1)
                link(TT(SsS[:, :, :], bank[2][:, :].rearrange("p (c d) -> p c d", c=NB),
                        X["Ep"][:, SEQ + NS - 1:NT:NS].unsqueeze(2).to_broadcast([128, NB, 64]), ALU.mult))
                TT(SsS[:, :, :], SsS[:, :, :], PHS[:, :, :], ALU.add).then_inc(S("rstate_ready"), 1)
                own(S("rstate_ready"))
                dve.wait_ge(S("y_inter"), p + 1)
                dve.wait_ge(S("y0_ready"), c_gh)
                link(TT(X["y"][:, RCH:SEQ], bank[3][:, RCH:SEQ], X["y"][:, RCH:SEQ], ALU.add))
                TT(X["y"][:, SEQ:NT], bank[4][:, 0:SAMP], X["y"][:, SEQ:NT], ALU.add).then_inc(S("y_full"), 1)
                own(S("y_full"))
                dve.wait_ge(S("gmean_done"), p + 1)
                for dst, src in zip(main_samp(X["y"]), (bank[5][:, :], bank[6][:, 0:SAMP])):
                    link(STT(out=dst, in0=src, scalar=-1.0 / 64, in1=dst, op0=ALU.mult, op1=ALU.add))
                TT(X["kk"][:, :], X["y"][:, :], X["y"][:, :], ALU.mult).then_inc(S("gsq_ready"), 1)
                own(S("gsq_ready"))
                dve.wait_ge(S("gstd_ready"), p + 1)
                link(dve.reciprocal(X["d"][:, :], X["d"][:, :]))
                link(STT(out=X["y"][:, :], in0=X["y"][:, :], scalar=pcol("gn_g", p), in1=X["d"][:, :], op0=ALU.mult, op1=ALU.mult))
                link(STT(out=X["y"][:, :], in0=X["y"][:, :], scalar=pcol("gn_b", p), in1=X["bv"][:, :], op0=ALU.add, op1=ALU.add))
                TT(mixT[:, 4 + p, :], X["y"][:, :], X["gv"][:, :], ALU.mult).then_inc(S("mix_ready"), 1)
                own(S("mix_ready"))
                dve.wait_ge(S("mix_ready"), 5 + p)
            dve.wait_ge(s_x1, 16 * 6)
            for half in range(2):
                for t, (t0, n) in enumerate(TILES):
                    jj = 5 * half + t
                    cs = slice(512 * half, 512 * half + 512)
                    dve.wait_ge(S("outproj_done"), jj + 1)
                    TT(x1[0:n, t, cs], bank[jj % 4][0:n, :], x1[0:n, t, cs], ALU.add).then_inc(S("x1_ready"), 1)
                    own(S("x1_ready"))
            for t, (t0, n) in enumerate(TILES):
                dve.wait_ge(S("frms_ready"), t + 1)
                link(dve.reciprocal(st[0:n, t, 1:2], st[0:n, t, 1:2]))
                if t >= 2:
                    dve.wait_ge(S("xfT_done"), t - 1)
                STT(out=xf[0:n, t % 2, :], in0=x1[0:n, t, :], scalar=st[0:n, t, 1:2], in1=gain[0:n, :], op0=ALU.mult, op1=ALU.mult
                    ).then_inc(S("xf_ready"), 1)
                own(S("xf_ready"))
            dve.wait_ge(S("iota_ready"), 1)

            def top16(val, ind, src, tmp):
                link(dve.max(val[:, 0:8], src))
                link(dve.max_index(ind[:, 0:8], val[:, 0:8], src))
                link(dve.match_replace(tmp, val[:, 0:8], src, -3.0e38))
                link(dve.max(val[:, 8:16], tmp))
                link(dve.max_index(ind[:, 8:16], val[:, 8:16], tmp))

            def one_hots(t):
                t0, n = TILES[t]
                dve.wait_ge(S("hk_done"), t + 1)
                link(dve.tensor_copy(hkT[:, :, 0:n], bank[4][:, 0:3 * n].rearrange("p (a n) -> p a n", a=3)))
                link(dve.tensor_copy(hk_hi[:, 0:n], hkT[:, 2, 0:n]))
                hi = hk_hi[:, :].bitcast(f32)
                TT(hkT[:, 2, 0:n], hkT[:, 2, 0:n], hi[:, 0:n], ALU.subtract).then_inc(S("hk_ready"), 1)
                own(S("hk_ready"))
                for j in range(n):
                    tok = t0 + j
                    if tok >= 8 and tok % 4 == 0:
                        dve.wait_ge(S("gmat_done"), tok // 4 - 1)
                    if tok % 4 == 3:
                        TS_(hot_b[:, tok % 8, :], io128[:, :], hkT[:, 1, j:j + 1], None, ALU.is_equal)
                    for part, g in enumerate((hi[:, j:j + 1], hkT[:, 2, j:j + 1])):
                        ins = TS_(hot_a[:, part, tok % 8, :], io128[:, :], hkT[:, 0, j:j + 1], g, ALU.is_equal, ALU.mult)
                    if tok % 4 == 3:
                        ins.then_inc(S("hot_a_ready"), 1)
                dve.wait_ge(S("hot_a_ready"), (t0 + n) // 4)
                dve.wait_ge(S("hot_b_ready"), (t0 + n) // 4)

            def route_tile(t):
                t0, n = TILES[t]
                sc = sca[:, t, :]
                dve.wait_ge(S("scores_ready"), t + 1)
                for j in range(16):
                    top16(sv[0:n, j, :], si[0:n, j, :], sc[0:n, 128 * j:128 * j + 128], sc2[0:n, 0:128])
                link(dve.tensor_copy(sif[0:n, :, :], si[0:n, :, :]))
                for h in range(HEADS):
                    link(TT(sc[0:n, 256 * h:256 * h + 256].rearrange("p (a b) -> p a b", a=16),
                            sv[0:n, 2 * h, :].unsqueeze(2).to_broadcast([n, 16, 16]),
                            sv[0:n, 2 * h + 1, :].unsqueeze(1).to_broadcast([n, 16, 16]), ALU.add))
                for h in range(HEADS):
                    top16(cv[0:n, h, :], ci[0:n, h, :], sc[0:n, 256 * h:256 * h + 256], sc2[0:n, :])
                gt = gate[0:n, t, :].rearrange("p (h k) -> p h k", h=HEADS)
                TT(gt, cv[0:n, :, :], cv[0:n, :, 0:1].to_broadcast([n, HEADS, 16]), ALU.subtract).then_inc(S("shifted"), 1)
                own(S("shifted"))
                cif = ci[0:n, :, :].rearrange("p h k -> p (h k)")
                link(TS_(cab[0:n, 0, :], cif, 4, None, ALU.logical_shift_right))
                link(TS_(cab[0:n, 1, :], cif, 15, None, ALU.bitwise_and))
                link(dve.tensor_copy(cabf[0:n, :, :], cab[0:n, :, :]))
                for side in range(2):
                    hot = sc[0:n, :].rearrange("p (k j) -> p k j", j=16)
                    link(TT(hot, cabf[0:n, side, :].unsqueeze(2).to_broadcast([n, 128, 16]),
                            io16[0:n, :].unsqueeze(1).to_broadcast([n, 128, 16]), ALU.is_equal))
                    hot4 = sc[0:n, :].rearrange("p (h k j) -> p h k j", h=HEADS, k=16)
                    link(TT(hot4, hot4, sif[0:n, side:16:2, :].unsqueeze(2).to_broadcast([n, HEADS, 16, 16]), ALU.mult))
                    link(dve.tensor_reduce(isel[0:n, side, :], hot, AX.X, ALU.add))
                dve.wait_ge(S("gexp_ready"), t + 1)
                link(dve.tensor_reduce(mx8[0:n, 0, :], gt, AX.X, ALU.add))
                link(dve.reciprocal(mx8[0:n, 1, :], mx8[0:n, 0, :]))
                TT(gt, gt, mx8[0:n, 1, :].unsqueeze(2).to_broadcast([n, HEADS, 16]), ALU.mult).then_inc(S("routed"), 1)
                own(S("routed"))

            dve.wait_ge(S("xhi_ready"), 1)
            TT(xlo[:, :, :], xfT[:, :, :], xhi[:, :, :].bitcast(f32), ALU.subtract).then_inc(S("xlo_ready"), 1)
            for t in range(5):
                route_tile(t)
                one_hots(t)
            dve.wait_ge(S("dots_done"), 2 * GU + GU * UG)
            link(dve.memset(acc[:, :, :], 0.0))
            dve.sem_inc(S("sum_banks_free"), 4)

            def weights(i, q):
                dve.wait_ge(s_grp[q], i * 32 + 32)
                for e in range(GE):
                    w = wts[:, q, e, :].rearrange("p (c t) -> p c t", c=NCH)
                    ins = TT(w, w, gring[:, q, :, e, :], ALU.mult)
                ins.then_inc(S("weights_ready"), 1)

            def split_weights(i, q):
                dve.wait_ge(S("w_hi_ready"), i * 2 + (q + 1))
                TT(w_lo[:, q, :, :], wts[:, q, :, :], w_hi[:, q, :, :].bitcast(f32), ALU.subtract).then_inc(S("w_lo_ready"), 1)

            def add_up(i, q, c):
                b = 2 * (c % 4)
                dve.wait_ge(S("sum_done"), i * 16 + (2 * KD + 8 * q + c + 1))
                dve.wait_ge(S("sum_banks_free"), i * 16 + max(8 * q + c - 3, 1))
                TT(acc[:, c, 0:HN], bank[b][:, 0:HN], acc[:, c, 0:HN], ALU.add)
                TT(acc[:, c, HN:NT], bank[b + 1][:, 0:HN], acc[:, c, HN:NT], ALU.add).then_inc(S("sum_banks_free"), 1)

            def turn(i, q, more=True):
                if more:
                    weights(i + q, 1 - q)
                for c in range(KD):
                    if c == 2 and more:
                        split_weights(i + q, 1 - q)
                    add_up(i, q, c)

            weights(0, 0)
            split_weights(0, 0)
            with dve.Fori(0, EG // 2 - 1) as i:
                turn(i, 0)
                turn(i, 1)
            turn(EG // 2 - 1, 0)
            turn(EG // 2 - 1, 1, more=False)
            dve.wait_ge(s_x1, 16 * 12)
            for t, (t0, n) in enumerate(TILES):
                dve.wait_ge(S("back_done"), t + 1)
                for half in range(2):
                    cs = slice(512 * half, 512 * half + 512)
                    last = TT(x1_late[0:n, t, cs], bank[2 * (t % 4) + half][0:n, :], x1_late[0:n, t, cs], ALU.add)
                last.then_inc(S("x2_ready"), 1)
                own(S("x2_ready"))
                dve.wait_ge(S("yrms_ready"), t + 1)
                link(dve.reciprocal(st[0:n, t, 3:4], st[0:n, t, 3:4]))
                STT(out=x1_late[0:n, t, :], in0=x1_late[0:n, t, :], scalar=st[0:n, t, 3:4], in1=gain[0:n, :], op0=ALU.mult, op1=ALU.mult
                    ).then_inc(S("y_ready"), 1)
                own(S("y_ready"))


_OUTS = [("y", (NT, D)), ("cn_p", (128, MLH, 129)), ("m", (4, 1 + NB)), ("conv", (128, 8, 1 + NB, 3)),
         ("s_p", (128, 4, 64)), ("shift", (128, RT_TILES, 1 + NB)), ("cn_s", (128, MLH, NB, 129)),
         ("s_s", (128, 4, NB, 64))]


def kernel(**inputs):
    import numpy as np
    import concourse.bacc as bacc
    from concourse.bass_utils import run_bass_kernel_spmd

    I = {k: np.asarray(v) for k, v in inputs.items()}
    tiles = lambda a: np.asarray(a).reshape(-1, 128).T
    x = np.concatenate([I["x_prompt"].reshape(SEQ, D), I["x_sample"].reshape(SAMP, D)])
    par = np.concatenate(
        [tiles(I["norm_mix_g"][0]), tiles(I["ml_conv_w"][0]), tiles(I["ml_conv_b"][0]), tiles(I["ml_norm_g"][0]),
         tiles(I["rw_mu"][0]), tiles(I["rw_w0"][0]), tiles(I["rw_a0"][0]), tiles(I["rw_k_k"][0]), tiles(I["rw_k_a"][0]),
         tiles(I["rw_r_k"][0]), tiles(I["rw_gn_g"][0]), tiles(I["rw_gn_b"][0])], axis=1)
    small = np.concatenate([I["ml_b_i"].T, I["ml_b_f"].T, I["state_mlstm_m"][0].T], axis=1)
    conv0 = I["state_mlstm_conv"][0].reshape(NB, 3, 8, 128).transpose(3, 2, 0, 1)
    shift0 = I["state_rwkv_shift"][0].reshape(NB, RT_TILES, 128).transpose(2, 1, 0)
    cn0 = np.concatenate([I["state_mlstm_C"][0].transpose(2, 0, 1, 3), I["state_mlstm_n"][0].transpose(2, 0, 1)[..., None]], axis=3)
    s0 = I["state_rwkv_S"][0].reshape(NB, 4, 2, 64, 64).transpose(2, 4, 0, 1, 3).reshape(128, NB, 4, 64)
    sub = I["peer_sub_keys"][0].reshape(16, 128, 128).transpose(2, 0, 1)
    pu = I["peer_u"][0].reshape(UG, GU * 128, KD, 128).transpose(0, 3, 2, 1)
    pv = I["peer_v"][0].reshape(EG, GE, 128, D).transpose(0, 2, 1, 3).reshape(EG, 128, GE * D)
    ins = [("xT", x.T), ("x", x), ("par", par), ("small", small), ("conv0", conv0), ("shift0", shift0), ("cn0", cn0),
           ("s0", s0), ("w_in", I["w_in"][0]), ("w2", I["rw_w2"][0]), ("a2", I["rw_a2"][0]), ("g2", I["rw_g2"][0]),
           ("w_out", I["w_out"][0]), ("gffn", I["norm_ffn_g"][0]), ("gfin", I["norm_final_g"]),
           ("w_q", I["peer_w_q"][0]), ("sub", sub), ("pu", pu), ("pv", pv)]
    nc = bacc.Bacc("TRN2", target_bir_lowering=False, num_devices=1)
    arrays, args = {}, []
    for name, a in ins:
        a = np.ascontiguousarray(a)
        arrays["in_" + name] = a
        args.append(nc.dram_tensor("in_" + name, a.shape, mybir.dt.from_np(a.dtype), kind="ExternalInput").ap())
    for name, shape in _OUTS:
        args.append(nc.dram_tensor("out_" + name, shape, mybir.dt.float32, kind="ExternalOutput").ap())
    hybrid_step(nc, *args)
    r = run_bass_kernel_spmd(nc, [arrays], core_ids=[0])
    o = {name: r.results[0]["out_" + name] for name, _ in _OUTS}
    cnp = o["cn_p"].transpose(1, 0, 2)
    cns = o["cn_s"].transpose(2, 1, 0, 3)
    conv = o["conv"].transpose(2, 3, 1, 0).reshape(1 + NB, 3, 1024)
    shift = o["shift"].transpose(2, 1, 0).reshape(1 + NB, RT_TILES * 128)
    unpair = lambda s: s.reshape(2, 64, 4, -1, 64).transpose(3, 2, 0, 4, 1).reshape(-1, 8, 64, 64)
    m = o["m"].T
    c = np.ascontiguousarray
    return (c(o["y"][0:SEQ].reshape(1, SEQ, D)), c(o["y"][SEQ:].reshape(NB, NS, D)),
            c(cnp[None, None, :, :, 0:128]), c(cnp[None, None, :, :, 128]), c(m[None, 0:1]), c(conv[None, 0:1]),
            c(unpair(o["s_p"])[None]), c(shift[None, 0:1]),
            c(cns[None, :, :, :, 0:128]), c(cns[None, :, :, :, 128]), c(m[None, 1:]), c(conv[None, 1:]),
            c(unpair(o["s_s"])[None]), c(shift[None, 1:]))
```
